# Optimizing a Trainium2 kernel written in Bass

```python
import math
import jax, jax.numpy as jnp
from jax import lax
import numpy as np

D_MODEL = 1024
BATCH = 1
SEQ = 128
DEPTH = 1
DEC_BATCH = 1
DEC_SEQ = 512
PAST_LEN = 128

GRID_W = 64
EPS = 1e-6
POOL_WIDTH = 256
POOL_GROUPS = 4
POOL_WINDOWS = (2, 4, 8, 16)
HYENA_WIDTH = 256
HYENA_BANDS = 16
HYENA_EMB = 1 + 2 * HYENA_BANDS
HYENA_FFN = 64
SCONV_WIDTH = 256
NA_HEADS = 8
NA_HEAD_DIM = 64
NA_WIDTH = NA_HEADS * NA_HEAD_DIM
NA_ROWS = 8
NA_COLS = 16
QBLK_COLS = 16
KBLK_COLS = 32
CTX_QBLK = 128
N_BRANCH = 4
IN_WIDTH = POOL_WIDTH + 3 * HYENA_WIDTH + 3 * SCONV_WIDTH + 3 * NA_WIDTH
MOE_GROUPS = 4
MOE_EXPERTS_PER_GROUP = 8
MOE_TOP_K = 2
MOE_D_FF = 256

kernel_name = 'hybrid_dit_step'

def _rmsnorm(x, g):
    xf = x.astype(jnp.float32)
    y = xf * lax.rsqrt(jnp.mean(xf * xf, axis=-1, keepdims=True) + EPS)
    return (y * g.astype(jnp.float32)).astype(x.dtype)

def _conv3(u, w):
    up = jnp.pad(u, ((0, 0), (1, 1), (0, 0)))
    return w[0] * up[:, :-2] + w[1] * up[:, 1:-1] + w[2] * up[:, 2:]

def _pool_mixer(u, pool_w, pool_scale):
    L = u.shape[1]
    uf = u.astype(jnp.float32)
    cs = jnp.pad(jnp.cumsum(uf, axis=1), ((0, 0), (1, 0), (0, 0)))
    t = np.arange(L)
    gw = POOL_WIDTH // POOL_GROUPS
    outs = []
    for g, win in enumerate(POOL_WINDOWS):
        lo = np.clip(t - win // 2, 0, L)
        hi = np.clip(t - win // 2 + win, 0, L)
        seg = cs[:, :, g * gw:(g + 1) * gw]
        cnt = jnp.asarray((hi - lo)[None, :, None], jnp.float32)
        pooled = (seg[:, hi] - seg[:, lo]) / cnt - uf[:, :, g * gw:(g + 1) * gw]
        outs.append(jnp.einsum('blc,ce->ble', pooled, pool_w[g].astype(jnp.float32)))
    y = jnp.concatenate(outs, axis=-1) * pool_scale.astype(jnp.float32)
    return y.astype(u.dtype)

def _hyena_filter(L, f1, fb1, f2, fb2, f3, freq, decay):
    f32 = jnp.float32
    t = jnp.arange(L, dtype=f32)
    w = (2.0 * math.pi / L) * t
    bands = jnp.linspace(1e-4, HYENA_BANDS - 1, HYENA_BANDS, dtype=f32)
    z = jnp.concatenate([(t / (L - 1))[:, None], jnp.cos(w[:, None] * bands),
                         -jnp.sin(w[:, None] * bands)], axis=-1)
    fr = freq.astype(f32)
    hdn = jnp.sin(fr * (z @ f1.astype(f32) + fb1.astype(f32)))
    hdn = jnp.sin(fr * (hdn @ f2.astype(f32) + fb2.astype(f32)))
    filt = hdn @ f3.astype(f32)
    dist = jnp.abs(t - (L // 2)) / (L / 2)
    filt = filt * jnp.exp(-dist[:, None] * decay.astype(f32)[None, :])
    return filt / jnp.sum(jnp.abs(filt), axis=0, keepdims=True)

def _hyena_mixer(p, conv_w, f1, fb1, f2, fb2, f3, freq, decay, bias):
    L = p.shape[1]
    x0, x1, v = jnp.split(_conv3(p, conv_w), 3, axis=-1)
    u = (x1 * v).astype(jnp.float32)
    h = _hyena_filter(L, f1, fb1, f2, fb2, f3, freq, decay)
    n = 2 * L
    spec = jnp.fft.rfft(u, n=n, axis=1) * jnp.fft.rfft(h, n=n, axis=0)[None]
    conv = jnp.fft.irfft(spec, n=n, axis=1)[:, L // 2:L // 2 + L]
    y = (conv + bias.astype(jnp.float32) * u) * x0.astype(jnp.float32)
    return y.astype(p.dtype)

def _shortconv_mixer(p, w):
    xc, bg, cg = jnp.split(p, 3, axis=-1)
    return bg * _conv3(cg * xc, w)

def _context_attention(q, k, v):
    B, Tc, H, d = q.shape
    scale = d ** -0.5
    nblk = Tc // CTX_QBLK
    qb = q.reshape(B, nblk, CTX_QBLK, H, d).transpose(1, 0, 2, 3, 4)

    def blk(qi):
        s = jnp.einsum('bqhd,bkhd->bhqk', qi, k, preferred_element_type=jnp.float32) * scale
        pr = jax.nn.softmax(s, axis=-1)
        return jnp.einsum('bhqk,bkhd->bqhd', pr.astype(v.dtype), v)

    o = lax.map(blk, qb)
    return o.transpose(1, 0, 2, 3, 4).reshape(B, Tc, H * d)

def _latent_attention(q, k, v, ctx_k, ctx_v, rpb):
    B, T, H, d = q.shape
    rows = T // GRID_W
    kr = min(NA_ROWS, rows)
    scale = d ** -0.5
    qg = q.reshape(B, rows, GRID_W, H, d)
    kg = k.reshape(B, rows, GRID_W, H, d)
    vg = v.reshape(B, rows, GRID_W, H, d)
    n_cb = GRID_W // QBLK_COLS
    q_col = np.arange(GRID_W).reshape(n_cb, QBLK_COLS)
    kcol_start = np.clip(np.arange(n_cb) * QBLK_COLS - (KBLK_COLS - QBLK_COLS) // 2, 0, GRID_W - KBLK_COLS)
    k_col = kcol_start[:, None] + np.arange(KBLK_COLS)[None, :]
    win_start = np.clip(q_col - NA_COLS // 2, 0, GRID_W - NA_COLS)
    kc = k_col[:, None, :]
    col_ok = jnp.asarray((kc >= win_start[:, :, None]) & (kc < win_start[:, :, None] + NA_COLS))
    dc_idx = np.clip(kc - q_col[:, :, None] + NA_COLS - 1, 0, 2 * NA_COLS - 2)
    rpb_c = rpb.astype(jnp.float32)[:, :, dc_idx]
    n_loc = kr * KBLK_COLS

    def row_fn(r):
        rs = jnp.clip(r - kr // 2, 0, rows - kr)
        k_blk = lax.dynamic_slice_in_dim(kg, rs, kr, axis=1)[:, :, k_col]
        v_blk = lax.dynamic_slice_in_dim(vg, rs, kr, axis=1)[:, :, k_col]
        q_blk = lax.dynamic_index_in_dim(qg, r, axis=1, keepdims=False).reshape(B, n_cb, QBLK_COLS, H, d)
        s_loc = jnp.einsum('bnqhd,bknjhd->bhnqkj', q_blk, k_blk, preferred_element_type=jnp.float32) * scale
        dr = rs + jnp.arange(kr) - r + (NA_ROWS - 1)
        bias = rpb_c[:, dr].transpose(0, 2, 3, 1, 4)
        s_loc = jnp.where(col_ok[None, None, :, :, None, :], s_loc + bias[None], -jnp.inf)
        s_loc = s_loc.reshape(B, H, n_cb, QBLK_COLS, n_loc)
        s_ctx = jnp.einsum('bnqhd,bchd->bhnqc', q_blk, ctx_k, preferred_element_type=jnp.float32) * scale
        pr = jax.nn.softmax(jnp.concatenate([s_loc, s_ctx], axis=-1), axis=-1).astype(v.dtype)
        p_loc = pr[..., :n_loc].reshape(B, H, n_cb, QBLK_COLS, kr, KBLK_COLS)
        o = (jnp.einsum('bhnqkj,bknjhd->bnqhd', p_loc, v_blk)
             + jnp.einsum('bhnqc,bchd->bnqhd', pr[..., n_loc:], ctx_v))
        return o.reshape(B, GRID_W, H, d)

    out = lax.map(row_fn, jnp.arange(rows))
    return out.transpose(1, 0, 2, 3, 4).reshape(B, T, H * d)

def _mixing(h, ctx_kv, P, l):
    B, L, _ = h.shape
    p = jnp.einsum('bld,de->ble', h, P['w_in'][l])
    o1 = POOL_WIDTH
    o2 = o1 + 3 * HYENA_WIDTH
    o3 = o2 + 3 * SCONV_WIDTH
    ya = _pool_mixer(p[..., :o1], P['pool_w'][l], P['pool_scale'][l])
    yb = _hyena_mixer(p[..., o1:o2], P['hyena_conv'][l], P['hyena_f1'][l], P['hyena_fb1'][l],
                      P['hyena_f2'][l], P['hyena_fb2'][l], P['hyena_f3'][l], P['hyena_freq'][l],
                      P['hyena_decay'][l], P['hyena_bias'][l])
    yc = _shortconv_mixer(p[..., o2:o3], P['sconv_w'][l])
    q, k, v = [t.reshape(B, L, NA_HEADS, NA_HEAD_DIM) for t in jnp.split(p[..., o3:], 3, axis=-1)]
    if ctx_kv is None:
        yd = _context_attention(q, k, v)
    else:
        yd = _latent_attention(q, k, v, ctx_kv[0], ctx_kv[1], P['na_rpb'][l])
    gates = jax.nn.sigmoid(jnp.einsum('bld,de->ble', h, P['w_gate'][l]) + P['b_gate'][l])
    ga, gb, gc, gd = jnp.split(gates, N_BRANCH, axis=-1)
    merged = (ga * (ya @ P['w_br_a'][l]) + gb * (yb @ P['w_br_b'][l])
              + gc * (yc @ P['w_br_c'][l]) + gd * (yd @ P['w_br_d'][l]))
    return merged @ P['w_out'][l], (k, v)

def _moe(h, P, l):
    B, L, D = h.shape
    x = h.reshape(B * L, D)
    gl = (x @ P['w_route_group'][l] + P['b_route_group'][l]).astype(jnp.float32)
    g_prob, g_idx = lax.top_k(jax.nn.softmax(gl, axis=-1), 1)
    g_sel = jax.nn.one_hot(g_idx[:, 0], MOE_GROUPS, dtype=jnp.float32)
    el = (jnp.einsum('td,gde->tge', x, P['w_route_exp'][l]) + P['b_route_exp'][l]).astype(jnp.float32)
    el_sel = jnp.einsum('tge,tg->te', el, g_sel)
    e_prob, e_idx = lax.top_k(jax.nn.softmax(el_sel, axis=-1), MOE_TOP_K)
    e_prob = e_prob / jnp.sum(e_prob, axis=-1, keepdims=True)
    w_exp = jnp.sum(jax.nn.one_hot(e_idx, MOE_EXPERTS_PER_GROUP, dtype=jnp.float32) * e_prob[..., None], axis=1) * g_prob
    combine = (g_sel[:, :, None] * w_exp[:, None, :]).astype(h.dtype)
    y = jnp.zeros_like(x)
    for g in range(MOE_GROUPS):
        a = jnp.einsum('td,edf->tef', x, P['w_e_gate'][l, g])
        b = jnp.einsum('td,edf->tef', x, P['w_e_up'][l, g])
        hid = jax.nn.silu(a) * b * combine[:, g, :, None]
        y = y + jnp.einsum('tef,efd->td', hid, P['w_e_down'][l, g])
    return y.reshape(B, L, D)

def _layer(x, cvec, ctx_kv, P, l):
    ada = jax.nn.silu(cvec) @ P['w_ada'][l] + P['b_ada'][l]
    sh1, sc1, g1, sh2, sc2, g2 = jnp.split(ada, 6, axis=-1)
    h = _rmsnorm(x, P['norm_mix'][l]) * (1.0 + sc1[:, None]) + sh1[:, None]
    mix, kv = _mixing(h, ctx_kv, P, l)
    x = x + g1[:, None] * mix
    h2 = _rmsnorm(x, P['norm_ffn'][l]) * (1.0 + sc2[:, None]) + sh2[:, None]
    x = x + g2[:, None] * _moe(h2, P, l)
    return x, kv

def setup_inputs(seed: int = 0) -> dict:
    key = jax.random.key(seed)
    ks = iter(jax.random.split(key, 48))
    f32 = jnp.float32

    def nrm(shape, scale):
        return jax.random.normal(next(ks), shape, f32) * scale

    D = D_MODEL
    PG = POOL_WIDTH // POOL_GROUPS
    G, E, F = MOE_GROUPS, MOE_EXPERTS_PER_GROUP, MOE_D_FF
    inp = {}
    inp['x_prompt'] = nrm((BATCH, SEQ, D), 1.0)
    inp['x_sample'] = nrm((DEC_BATCH, DEC_SEQ, D), 1.0)
    inp['cache_k'] = nrm((DEC_BATCH, DEPTH, PAST_LEN, NA_HEADS, NA_HEAD_DIM), 1.0)
    inp['cache_v'] = nrm((DEC_BATCH, DEPTH, PAST_LEN, NA_HEADS, NA_HEAD_DIM), 1.0)
    inp['c'] = nrm((DEC_BATCH, D), 1.0)
    inp['c_ctx'] = nrm((D,), 1.0)
    inp['w_ada'] = nrm((DEPTH, D, 6 * D), 0.5 * D ** -0.5)
    inp['b_ada'] = nrm((DEPTH, 6 * D), 0.1)
    inp['norm_mix'] = 1.0 + nrm((DEPTH, D), 0.1)
    inp['w_in'] = nrm((DEPTH, D, IN_WIDTH), D ** -0.5)
    inp['w_gate'] = nrm((DEPTH, D, N_BRANCH * D), D ** -0.5)
    inp['b_gate'] = nrm((DEPTH, N_BRANCH * D), 0.1)
    inp['pool_w'] = nrm((DEPTH, POOL_GROUPS, PG, PG), PG ** -0.5)
    inp['pool_scale'] = 1.0 + nrm((DEPTH, POOL_WIDTH), 0.1)
    inp['hyena_conv'] = nrm((DEPTH, 3, 3 * HYENA_WIDTH), 0.5)
    inp['hyena_f1'] = nrm((DEPTH, HYENA_EMB, HYENA_FFN), HYENA_EMB ** -0.5)
    inp['hyena_fb1'] = nrm((DEPTH, HYENA_FFN), 0.1)
    inp['hyena_f2'] = nrm((DEPTH, HYENA_FFN, HYENA_FFN), HYENA_FFN ** -0.5)
    inp['hyena_fb2'] = nrm((DEPTH, HYENA_FFN), 0.1)
    inp['hyena_f3'] = nrm((DEPTH, HYENA_FFN, HYENA_WIDTH), HYENA_FFN ** -0.5)
    inp['hyena_freq'] = 1.0 + nrm((DEPTH, HYENA_FFN), 0.1)
    inp['hyena_decay'] = jnp.exp(jax.random.uniform(next(ks), (DEPTH, HYENA_WIDTH), f32,
                                                    math.log(3.0), math.log(15.0)))
    inp['hyena_bias'] = nrm((DEPTH, HYENA_WIDTH), 0.5)
    inp['sconv_w'] = nrm((DEPTH, 3, SCONV_WIDTH), 0.5)
    inp['na_rpb'] = nrm((DEPTH, NA_HEADS, 2 * NA_ROWS - 1, 2 * NA_COLS - 1), 0.2)
    inp['w_br_a'] = nrm((DEPTH, POOL_WIDTH, D), POOL_WIDTH ** -0.5)
    inp['w_br_b'] = nrm((DEPTH, HYENA_WIDTH, D), HYENA_WIDTH ** -0.5)
    inp['w_br_c'] = nrm((DEPTH, SCONV_WIDTH, D), SCONV_WIDTH ** -0.5)
    inp['w_br_d'] = nrm((DEPTH, NA_WIDTH, D), NA_WIDTH ** -0.5)
    inp['w_out'] = nrm((DEPTH, D, D), D ** -0.5)
    inp['norm_ffn'] = 1.0 + nrm((DEPTH, D), 0.1)
    inp['w_route_group'] = nrm((DEPTH, D, G), D ** -0.5)
    inp['b_route_group'] = nrm((DEPTH, G), 0.01)
    inp['w_route_exp'] = nrm((DEPTH, G, D, E), D ** -0.5)
    inp['b_route_exp'] = nrm((DEPTH, G, E), 0.01)
    inp['w_e_gate'] = nrm((DEPTH, G, E, D, F), D ** -0.5)
    inp['w_e_up'] = nrm((DEPTH, G, E, D, F), D ** -0.5)
    inp['w_e_down'] = nrm((DEPTH, G, E, F, D), F ** -0.5)
    inp['norm_final'] = 1.0 + nrm((D,), 0.1)
    return inp

def reference(x_prompt, x_sample, cache_k, cache_v, c, c_ctx, w_ada, b_ada, norm_mix, w_in,
              w_gate, b_gate, pool_w, pool_scale, hyena_conv, hyena_f1, hyena_fb1, hyena_f2,
              hyena_fb2, hyena_f3, hyena_freq, hyena_decay, hyena_bias, sconv_w, na_rpb,
              w_br_a, w_br_b, w_br_c, w_br_d, w_out, norm_ffn, w_route_group, b_route_group,
              w_route_exp, b_route_exp, w_e_gate, w_e_up, w_e_down, norm_final):
    P = dict(w_ada=w_ada, b_ada=b_ada, norm_mix=norm_mix, w_in=w_in, w_gate=w_gate, b_gate=b_gate,
             pool_w=pool_w, pool_scale=pool_scale, hyena_conv=hyena_conv, hyena_f1=hyena_f1,
             hyena_fb1=hyena_fb1, hyena_f2=hyena_f2, hyena_fb2=hyena_fb2, hyena_f3=hyena_f3,
             hyena_freq=hyena_freq, hyena_decay=hyena_decay, hyena_bias=hyena_bias, sconv_w=sconv_w,
             na_rpb=na_rpb, w_br_a=w_br_a, w_br_b=w_br_b, w_br_c=w_br_c, w_br_d=w_br_d, w_out=w_out,
             norm_ffn=norm_ffn, w_route_group=w_route_group, b_route_group=b_route_group,
             w_route_exp=w_route_exp, b_route_exp=b_route_exp, w_e_gate=w_e_gate, w_e_up=w_e_up,
             w_e_down=w_e_down)
    xp = x_prompt
    c_p = jnp.broadcast_to(c_ctx[None, :], (x_prompt.shape[0], D_MODEL))
    k_list, v_list = [], []
    for l in range(DEPTH):
        xp, (k_l, v_l) = _layer(xp, c_p, None, P, l)
        k_list.append(k_l)
        v_list.append(v_l)
    y_prompt = _rmsnorm(xp, norm_final)
    new_k = jnp.stack(k_list, axis=1)
    new_v = jnp.stack(v_list, axis=1)
    xs = x_sample
    for l in range(DEPTH):
        xs, _ = _layer(xs, c, (cache_k[:, l], cache_v[:, l]), P, l)
    y_sample = _rmsnorm(xs, norm_final)
    return (y_prompt, y_sample, new_k, new_v)


_drawn_inputs = setup_inputs


def setup_inputs(seed=0):
    import zlib

    import numpy as np

    out = dict(_drawn_inputs(seed))
    spreads = {}
    factors = {'cache_k': 35.536,
     'cache_v': 29.184,
     'b_gate': 4.57,
     'pool_scale': 3.03,
     'hyena_fb1': 7.731,
     'hyena_fb2': 7.007,
     'hyena_freq': 8.0,
     'hyena_decay': 17.763,
     'na_rpb': 64.0,
     'b_route_group': 63.443,
     'b_route_exp': 20.355}
    for name, (base, spread) in spreads.items():
        noise = np.random.default_rng([zlib.crc32(name.encode()), seed]).standard_normal(out[name].shape)
        drawn = base * np.exp(spread * noise) if base else spread * noise
        out[name] = __import__('jax').numpy.asarray(drawn.astype(out[name].dtype))
    for name, factor in factors.items():
        out[name] = (out[name] * factor).astype(out[name].dtype)
    return out
```

```python
from contextlib import ExitStack

import numpy as np
import concourse.bass as bass
from concourse import mybir

F32 = mybir.dt.float32
U32 = mybir.dt.uint32
I32 = mybir.dt.int32
ALU = mybir.AluOpType
ACT = mybir.ActivationFunctionType
AX = mybir.AxisListType

P = 128
D = 1024
KD = D // P
TC, TL = 128, 512
T = TC + TL
NT = T // P
GRID_W = 64
HEADS, HD = 8, 64
NG, NE, FF = 4, 8, 256
EXPERTS = NG * NE
EPS = 1e-6
SCALE = HD ** -0.5
NEG = -1e30
PAD = 8
CPAD = PAD
LPAD = PAD + TC + PAD
WPAD = LPAD + TL + PAD
NBL, NBC = 3 * TL // 4, 3 * TC // 4
RPB_R, RPB_C = 15, 31
BROWS = 14
RPB_PAD = 64
CAP = 100
BLOCKS = -(-T // CAP)
LIST = BLOCKS * CAP
NPAIR = 2 * T
NOV = 16
W0 = 384

CW_ = 256
CHUNKS = [256, 512, 768, 1024, 1280, 1536, 0, 1792, 2048, 2304, 2560, 2816, 3072]
V_CHUNKS = (11, 12)
CHUNK_OF = {at // P + i: c for c, at in enumerate(CHUNKS) if c < 11 for i in range(2)}
SLOT = {t: n % 8 for n, t in enumerate([2, 3, 4, 5, 6, 7, 8, 9, 10, 11, 12, 13, 0, 1])}
BRANCHES = [(0, 0, 2), (2, 2, 2), (1, 1, 2), (3, 3, 4)]


def layout(items):
    at, out = 0, {}
    for name, n in items:
        out[name] = (at, at + n)
        at += n
    out["_"] = (0, at)
    return out


CB = layout([("ident", P), ("ones", P), ("before", P), ("window", GRID_W), ("negdist", NT), ("gid", NG),
             ("eid", NE), ("slot0", EXPERTS), ("pair", 2 * NT), ("invwin", 2), ("edge", 2 * 4 * PAD),
             ("eps", 1), ("thr", BLOCKS - 1), ("blk", 2 * (BLOCKS - 1)), ("iota", NOV), ("nopair", 1), ("place", CAP)])
CV = layout([("b_ada", 48), ("norm_mix", 8), ("b_gate", 32), ("norm_ffn", 8), ("pool_scale", 2),
             ("hyena_bias", 2), ("hyena_conv", 18), ("sconv_w", 6)])
CW = layout([("c", 16), ("fb1", 1), ("fb2", 1), ("freq", 1)])


def constants():
    f = np.float32
    blob = np.zeros((P, CB["_"][1]), f)

    def put(name, v):
        blob[:v.shape[0], CB[name][0]:CB[name][1]] = v

    i = np.arange(P)
    put("ident", np.eye(P))
    put("ones", np.ones((P, P)))
    put("before", i[:, None] < i[None, :])
    qc, kc = i[:, None] % GRID_W, np.arange(GRID_W)[None, :]
    ws = np.clip(qc - 8, 0, GRID_W - 16)
    put("window", np.where((kc >= ws) & (kc < ws + 16), 0.0, NEG))
    dist = np.concatenate([np.abs(np.arange(TC) - TC // 2) / (TC / 2), np.abs(np.arange(TL) - TL // 2) / (TL / 2)])
    put("negdist", -dist.reshape(NT, P).T)
    put("gid", np.tile(np.arange(NG) - 64.0, (P, 1)))
    put("eid", np.tile(np.arange(NE) - 64.0, (P, 1)))
    put("slot0", np.tile(np.arange(EXPERTS) * float(LIST), (P, 1)))
    put("pair", np.stack([s * T + t * P + i for s in range(2) for t in range(NT)], 1))
    win = np.array([[2, 8], [4, 16]])[i // 64]
    put("invwin", 1.0 / win)
    edge = np.ones((P, 2, 4, PAD))
    for s, L in enumerate((TC, TL)):
        for side in range(2):
            t = np.arange(PAD) + side * (L - PAD)
            w = win[:, :, None]
            cnt = np.clip(t - w // 2 + w, 0, L) - np.clip(t - w // 2, 0, L)
            edge[:, :, 2 * s + side] = w / cnt
    put("edge", edge.reshape(P, -1))
    put("eps", np.full((P, 1), EPS))
    put("thr", np.tile(CAP * (np.arange(BLOCKS - 1) + 1.0), (P, 1)))
    e, b = i[:32, None], np.arange(BLOCKS - 1)[None, :] + 1
    put("blk", np.stack([e + 0 * b, e * LIST + b * CAP], 2).reshape(32, -1))
    put("iota", np.tile(np.arange(NOV), (P, 1)))
    put("place", np.tile(np.arange(CAP), (P, 1)))
    put("nopair", np.full((P, 1), 2.0 * NPAIR))

    def odd_dft(L):
        n = 3 * L // 2
        a = 2 * np.pi * ((2 * np.arange(n // 2)[None, :] + 1) * np.arange(n)[:, None] % (2 * n)) / (2 * n)
        fwd = np.concatenate([np.cos(a[:L]), -np.sin(a[:L])], 1)
        b = a[L // 2:L // 2 + L].T * 1.0
        inv = np.concatenate([np.cos(b), -np.sin(b)], 0) * (2.0 / n)
        return fwd.astype(f), inv.astype(f)

    fl, il = odd_dft(TL)
    fc, ic = odd_dft(TC)
    icp = np.zeros((2, P, TC), f)
    icp[:, :NBC] = ic.reshape(2, NBC, TC)
    dft = np.concatenate([fl.reshape(4, P, 2 * NBL).transpose(1, 0, 2).reshape(P, -1), fc,
                          il.reshape(6, P, TL).transpose(1, 0, 2).reshape(P, -1),
                          icp.transpose(1, 0, 2).reshape(P, -1)], 1)

    def embed(L):
        t = np.arange(L, dtype=f)
        w = f(2.0 * np.pi / L) * t
        bands = np.linspace(1e-4, 15, 16, dtype=f)
        a = (w[:, None] * bands).astype(f)
        return np.concatenate([(t / f(L - 1))[:, None], np.cos(a), -np.sin(a)], 1).T

    z = np.concatenate([embed(TC), embed(TL)], 1).astype(f)
    lists = np.full((EXPERTS, LIST), 2.0 * NPAIR, f)
    return {"blob": blob, "dft": dft, "z": z, "lists": lists}


HALVES = {3 * i + h: (4 + i, h) for i in range(8) for h in range(2)}


def make_steps():
    s = [("vec", 1), ("ada", 0), ("f1",), ("ada", 1), ("f2",), ("vec", 0), ("adaT", 0), ("ada", 2), ("f3", 0), ("f3", 1),
         ("adaT", 1), ("ada", 3), ("nrm",), ("adaT", 2), ("adaT", 3)]
    s += [("xT", t) for t in range(NT)]
    s += [("p", t) for t in (2, 3, 4, 5, 6, 7, 8, 9, 10, 11)] + [("uT", 0), ("uT", 1)]
    s += [("p", t) for t in (12, 13, 0, 1)] + [("dft", k) for k in range(4)]
    s += [("p", t) for t in range(14, 22)] + [("pw", 0), ("pw", 1), ("idft", 0), ("idft", 1)]
    s += [("v", t) for t in range(NT)] + [("krow",), ("ckT",)]
    n = 0
    for b in range(len(BRANCHES)):
        for dj in range(KD):
            att = n < 4 * NT
            if att:
                s += [("S", 2 * n), ("S", 2 * n + 1)]
            if 0 < n <= 4 * NT:
                s += [("OT", n - 1)]
            s += [("gate", b, dj)]
            if n - 1 in HALVES:
                s += [("part",) + HALVES[n - 1]]
            if att:
                s += [("PT", 2 * n), ("PT", 2 * n + 1)]
            s += [("br", b, dj)]
            if att:
                s += [("O", n)]
            n += 1
        if b == 2:
            s += [("rows",)]
    for t in range(NT):
        s += [("out", t)]
        if t >= 1:
            s += [("hT", t - 1)]
        if t >= 2:
            s += [("route", t - 2)]
    s += [("hT", NT - 1), ("route", NT - 2), ("route", NT - 1)]
    s += [("pos",), ("count",), ("blocks",), ("further",), ("lists",)]
    return s


STEPS = make_steps()
AT = {s: n for n, s in enumerate(STEPS)}
assert len(AT) == len(STEPS)


def loads_of(step):
    k = step[0]
    if k == "ada":
        return [("ada", step[1], h) for h in range(2)]
    if k == "p":
        return [("win", CHUNK_OF[step[1]])]
    if k == "v":
        return [("win", c) for c in V_CHUNKS]
    if k == "gate":
        n = step[1] * KD + step[2]
        early = [("ada",) + HALVES[n]] if n in HALVES else []
        return early + [("gate", step[1], step[2] // 2)]
    if k == "part":
        return [("ada", step[1], step[2])]
    if k == "br":
        return [("branch", step[1], i) for i in range(BRANCHES[step[1]][2] // 2)]
    if k == "out":
        return [("wout", i) for i in range(KD // 2)]
    return []


RING, HELD = 4, 2
SLOTF = 2048
LAST = {}
for _s in STEPS:
    for _l in loads_of(_s):
        LAST[_l] = _s
LOADS = list(LAST.items())
PLACE, _used = {}, [[] for _ in range(RING + HELD)]
for _name, _last in LOADS:
    _held = _name[0] == "branch"
    _n = sum((x[0] == "branch") == _held for x in PLACE)
    _slot = RING + _n % HELD if _held else _n % RING
    PLACE[_name] = (_slot, len(_used[_slot]) + 1, _used[_slot][-1] if _used[_slot] else None)
    _used[_slot].append(_last)


def job(m):
    n = m // 2
    return 2 * (n // NT) + m % 2, n % NT


def build(nc, I, O):
    with ExitStack() as ctx:
        def sb(name, n, parts=P, dt=F32):
            return ctx.enter_context(nc.sbuf_tensor(name, [parts, n], dt))

        def sem(name):
            return ctx.enter_context(nc.semaphore(name))

        cb = sb("constants", CB["_"][1])
        colv = sb("colv", CV["_"][1])
        colw = sb("colw", CW["_"][1])
        ada = sb("ada", 48 * 2)
        mod = sb("mod", 8 * KD)
        scT = sb("scT", 16)
        small = sb("small", 64)
        ssq, rms, rstd = small[:, 10:15], small[:, 15:20], small[:, 20:25]
        negmax, expsum, rowmax, rsum = small[:, 25:27], small[:, 27:29], small[:, 29:31], small[:, 31:33]
        nrm = small[:, 33:37]
        a1 = small[:, 38:54].rearrange("p (k m) -> p k m", k=2)
        RA = sb("hT_region", KD * T)
        RR = sb("ring_region", (RING + HELD) * SLOTF)
        RY = sb("mixer_region", 6 * T)
        RQ = sb("qkv_region", 12 * T)
        RP = sb("padded_region", 8 * WPAD)
        RD = sb("dft_region", 8 * NBL + 2 * NBC + 6 * TL + 2 * TC)
        RB = sb("bias_region", 2 * BROWS * GRID_W)
        RH = sb("hyena_region", 8800)

        def c_(name, parts=P):
            return cb[0:parts, CB[name][0]:CB[name][1]]

        def v_(name):
            return colv[:, CV[name][0]:CV[name][1]]

        ident = c_("ident")
        hT = RA[:, :].rearrange("p (k t) -> p k t", k=KD)
        ring = [RR[:, SLOTF * s:SLOTF * (s + 1)] for s in range(RING + HELD)]
        yT = RY[:, :].rearrange("p (j t) -> p j t", t=T)
        yaT, ybT, ycT = yT[:, 0:2], yT[:, 2:4], yT[:, 4:6]
        pooled = ybT
        qT = RQ[:, 0:4 * T].rearrange("p (j t) -> p j t", t=T)
        kT = RQ[:, 4 * T:8 * T].rearrange("p (j t) -> p j t", t=T)
        vrow = RQ[:, 8 * T:12 * T].rearrange("p (t e) -> p t e", t=NT)
        xrow = RQ[:, 0:NT * D].rearrange("p (t d) -> p t d", t=NT)
        x1 = RQ[:, 4 * T:12 * T].rearrange("p (t d) -> p t d", t=NT)
        zt = RQ[0:33, NT * D:NT * D + T]
        f1s = RQ[0:33, NT * D + T:NT * D + T + 64]
        f2s = RQ[0:64, NT * D + T + 64:NT * D + T + 128]
        f3s = RQ[0:64, NT * D + T + 128:NT * D + T + 384]
        vrows = [RQ[:, NT * D + T + 384 + P * n:NT * D + T + 384 + P * (n + 1)] for n in range(2)]
        decay = RQ[:, NT * D + T + 640:NT * D + T + 896]
        pt = RP[:, :].rearrange("p (s t) -> p s t", s=8)
        fl_n = 4 * 2 * NBL
        adr = [RD[0:2, 512 * i:512 * (i + 1)] for i in range(2)]

        def ada_row(c):
            return adr[c % 2]

        apart = RH[:, 8192:8704].rearrange("p (h n) -> p h n", h=2)

        FLt = RD[:, 0:fl_n].rearrange("p (k f) -> p k f", k=4)
        FC = RD[:, fl_n:fl_n + 2 * NBC]
        il = fl_n + 2 * NBC
        IL = RD[:, il:il + 6 * TL].rearrange("p (k t) -> p k t", k=6)
        IC = RD[:, il + 6 * TL:il + 6 * TL + 2 * TC].rearrange("p (k t) -> p k t", k=2)
        merged = RD[:, 0:KD * T].rearrange("p (k t) -> p k t", k=KD)
        UF = RH[:, 0:2560].rearrange("p (t c) -> p t c", t=NT)
        hsp = RH[:, 2560:3072].rearrange("p (i c) -> p i c", i=2)
        tsp = RH[:, 3072:4096].rearrange("p (i c) -> p i c", i=4)
        cvt = RH[:, 2560:2560 + 2 * WPAD].rearrange("p (i t) -> p i t", i=2)
        ysp = RH[:, 4096:6144].rearrange("p (i c) -> p i c", i=8)
        env = RH[:, 4096:4096 + 1280].rearrange("p (t c) -> p t c", t=NT)
        x0 = RH[:, 6144:6144 + 2 * WPAD].rearrange("p (i t) -> p i t", i=2)
        uc = RH[:, 6144 + 2 * WPAD:6144 + 4 * WPAD].rearrange("p (i t) -> p i t", i=2)
        sn = RH[0:64, 6144:6144 + 4 * T].rearrange("p (i t) -> p i t", i=4)
        bias = [RB[:, BROWS * GRID_W * h:BROWS * GRID_W * (h + 1)] if h < 2 else
                RH[:, BROWS * GRID_W * (h - 2):BROWS * GRID_W * (h - 1)] for h in range(HEADS)]
        hb = 6 * BROWS * GRID_W
        ckr = RH[:, hb:hb + 512]
        cvr = RH[:, hb + 512:hb + 1024]
        ckT = RH[:, hb + 1024:hb + 1536].rearrange("p (j t) -> p j t", j=4)
        s_sb = RP[:, 0:2 * T].rearrange("p (i t) -> p i t", i=2)
        pT = RP[:, 2 * T:4 * T].rearrange("p (i k q) -> p i k q", i=2, k=NT)
        gate = RP[:, 4 * T:6 * T].rearrange("p (i t) -> p i t", i=2)
        gtmp = RP[:, 6 * T:7 * T]
        orow = RP[:, 7 * T:7 * T + P]
        krow = RP[:, 7 * T + P:7 * T + P + 512]
        rowb = RH[:, 0:8 * D].rearrange("p (i d) -> p i d", i=8)
        h2row = RY[:, 0:2 * D].rearrange("p (i d) -> p i d", i=2)
        junk = RY[:, 2 * D:3 * D]
        pwb = ctx.enter_context(nc.sbuf_tensor("pool_w_blocks", [P, 2, P], F32))
        wA = small[:, 0:5]
        wB = small[:, 5:10]
        wroute = RP[:, 0:KD * 36].rearrange("p (k n) -> p k n", k=KD)
        rbias = RP[:, 288:324]
        lg = RP[:, 324:504].rearrange("p (t n) -> p t n", t=NT)
        b0 = 504
        def take(n):
            nonlocal b0
            b0 += n
            return RP[:, b0 - n:b0]
        m32 = take(160).rearrange("p (t g e) -> p t g e", t=NT, g=NG)
        selA = take(160).rearrange("p (t g e) -> p t g e", t=NT, g=NG)
        selB = take(160).rearrange("p (t g e) -> p t g e", t=NT, g=NG)
        posb = take(160).rearrange("p (t n) -> p t n", t=NT)
        gx = [take(20).rearrange("p (t g) -> p t g", t=NT) for _ in range(3)]
        ex = [take(40).rearrange("p (t e) -> p t e", t=NT) for _ in range(5)]
        r5 = [take(5) for _ in range(12)]
        slotf = take(10)
        rankf = take(10)
        fl5 = take(2 * (BLOCKS - 1))
        ovs = take(NOV * (BLOCKS - 1))
        ovr = take(2 * NOV + 1)
        ovi = sb("further_lists", 2 * NOV + 1)
        cnt = take(2)
        idx = RB[:, 0:EXPERTS + 1]
        idxo = RB[:, 64:66]
        slotu = RB[:, 70:80]
        idxf = RB[:, 80:80 + EXPERTS]
        atplace = RB[:, 128:128 + 2 * NT * CAP].rearrange("p (n j) -> p n j", j=CAP)
        b1 = 128 + 2 * NT * CAP
        idsel = RB[:, b1:b1 + 320].rearrange("p (n e) -> p n e", e=EXPERTS)
        ranked = RB[:, b1 + 320:b1 + 480].rearrange("p (t e) -> p t e", e=EXPERTS)
        fin_n = RH[:, 2 * D:3 * D]

        pair_ps = [ctx.enter_context(nc.psum_tensor(f"pair{i}", [P, 1024], F32)) for i in range(4)]

        rows_d = nc.dram_tensor("mod_rows", [64, P], F32, kind="Internal").ap()
        hid_d = nc.dram_tensor("h2_pairs", [NPAIR, D], F32, kind="Internal").ap()
        out_d = nc.dram_tensor("moe_pairs", [NPAIR, D], F32, kind="Internal").ap()
        rpb_d = nc.dram_tensor("rpb_by_column", [HEADS * RPB_R, GRID_W, GRID_W], F32, kind="Internal").ap()
        list_d = nc.dram_tensor("slot_lists", [EXPERTS * LIST, 1], F32, kind="Internal").ap()

        psum_full = [sem(f"psum_full{i}") for i in range(4)]
        psum_free = [sem(f"psum_free{i}") for i in range(4)]
        ring_full = [sem(f"ring_full{i}") for i in range(RING + HELD)]
        blob_in, vecs_in, x_in, filt_in, dft_in, cache_in, bias01_in, bias_in, pw_in, route_in, nfin_in = (
            sem(n) for n in ("blob_in", "vecs_in", "x_in", "filt_in", "dft_in", "cache_in", "bias01_in", "bias_in",
                             "pw_in", "route_in", "nfin_in"))
        rows_out, rows_in, list_init, list_out, places_done = (
            sem(n) for n in ("rows_out", "rows_in", "list_init", "list_out", "places_done"))
        rpb_out, cond_in, ada_summed = sem("rpb_out"), sem("cond_in"), sem("modulation_summed")
        h2_out = [sem(f"h2_out{i}") for i in range(2)]
        x_again, kv_out, y_out = sem("x_again"), sem("kv_out"), sem("y_out")
        dve_own, act_own, pool_own = sem("dve_own"), sem("act_own"), sem("pool_own")
        (vec_done, scT_done, ssq_done, rms_done, xn_done, mod1_done, sin_in, sin_out, env_done, filt_done,
         abs_done, conv_done, u_done, hs_done, ysp_done, ya_pooled, yb_done, yc_done, padded_read, bias_ready01,
         bias_ready, exp_in, exp_out, merged_add, orow_done, mod_done, x1_done, ssq2_done, rms2_done,
         h2a_done, h2_done, gexp_in, gexp_out, mask_done, slots_done, flags_done, sel_done, list_ready) = (
            sem(n) for n in ("vec_done", "scT_done", "ssq_done", "rms_done", "xn_done", "mod1_done", "sin_in",
                             "sin_out", "env_done", "filt_done", "abs_done", "conv_done", "u_done", "hs_done",
                             "ysp_done", "ya_pooled", "yb_done", "yc_done", "padded_read", "bias_ready01",
                             "bias_ready", "exp_in", "exp_out", "merged_add", "orow_done", "mod_done",
                             "x1_done", "ssq2_done", "rms2_done", "h2a_done", "h2_done", "gexp_in", "gexp_out",
                             "mask_done", "slots_done", "flags_done", "sel_done", "list_ready"))

        def ps(step):
            return pair_ps[AT[step] % 4]

        def computed(eng, step):
            eng.wait_ge(psum_full[AT[step] % 4], AT[step] // 4 + 1)

        def drained(eng, step):
            eng.wait_ge(psum_free[AT[step] % 4], AT[step] // 4 + 1)

        def frees(ins, step):
            ins.then_inc(psum_free[AT[step] % 4], 1)

        def loaded(eng, name):
            slot, nth, _ = PLACE[name]
            eng.wait_ge(ring_full[slot], 16 * nth)
            return ring[slot]

        class Own:
            def __init__(self, eng, s):
                self.eng, self.s, self.n = eng, s, 0

            def put(self, ins):
                self.n += 1
                ins.then_inc(self.s, 1)

            def wait(self):
                self.eng.wait_ge(self.s, self.n)

            def link(self, ins):
                self.put(ins)
                self.wait()

        wsets = [(RR[:, 0:2048], RR[:, 2048:4096], RR[:, 4096:6144]),
                 (RR[:, 6144:8192], RR[:, 8192:10240], RR[:, 10240:12288]),
                 (RA[:, 0:2048], RA[:, 2048:4096], RD[:, 0:2048]),
                 (RD[:, 2048:4096], RD[:, 4096:6144], RH[:, 6144:8192])]
        wsets = [(a.rearrange("p (k f) -> p k f", k=KD), b.rearrange("p (k f) -> p k f", k=KD),
                  c.rearrange("p (k n) -> p k n", k=2)) for a, b, c in wsets]
        SETS = len(wsets)
        BUFS = 4
        xg = [RY[0:CAP, 0:D], RY[0:CAP, D:2 * D], RQ[0:CAP, D:2 * D], RH[0:CAP, 3 * D:4 * D]]
        sil = [RY[:, 2 * D + 256 * i:2 * D + 256 * (i + 1)].rearrange("p (f b) -> p f b", f=2) for i in range(2)]
        hid = [RY[:, 2 * D + 512 + 256 * i:2 * D + 512 + 256 * (i + 1)].rearrange("p (f b) -> p f b", f=2)
               for i in range(2)]
        xgT = [RP[:, D * i:D * (i + 1)].rearrange("p (k b) -> p k b", k=KD) for i in range(2)]
        yg = [RP[0:CAP, 2 * D:3 * D], RP[0:CAP, 3 * D:4 * D], RH[0:CAP, 4 * D:5 * D], RH[0:CAP, 5 * D:6 * D]]
        w_full = [sem(f"expert_weights{i}") for i in range(SETS)]
        wd_full = [sem(f"expert_second_weights{i}") for i in range(SETS)]
        xg_full = [sem(f"gathered{i}") for i in range(BUFS)]
        y_sent = [sem(f"scattered{i}") for i in range(BUFS)]
        xT_full, xT_free, gu_full, gu_free, dn_full, dn_free, sil_done = (
            sem(n) for n in ("moe_x_turned", "moe_x_drained", "moe_up_full", "moe_up_free", "moe_down_full",
                             "moe_down_free", "moe_silu_done"))
        scatters_done, pool_steps = sem("scatters_done"), sem("pool_steps")
        ov_idx_in, ov_idx_ready = sem("further_idx_in"), sem("further_idx_ready")
        ov_w = sem("further_weights")
        MX, MG, MD = pair_ps[0], pair_ps[1], pair_ps[2]
        fin_d = [RR[:, 2 * D * i:2 * D * (i + 1)].rearrange("p (s d) -> p s d", s=2) for i in range(NT)]
        fin_in = [sem(f"pair_rows_in{t}") for t in range(NT)]
        fin_first, fin_sum, fin_g2, fin_sq, fin_rms, fin_done = (
            sem(f"final_{n}") for n in ("first", "sum", "g2", "x2", "rms", "done"))

        block = ctx.enter_context(nc.Block())

        def n_further(eng):
            eng.wait_ge(list_ready, 1)
            return eng.value_load(ovi[0:1, 2 * NOV:2 * NOV + 1].bitcast(I32), min_val=0, max_val=NOV)

        @block.sync
        def _(sp):
            w_in, w_gate, w_out, w_ada = I["w_in"][0], I["w_gate"][0], I["w_out"][0], I["w_ada"][0]
            sp.dma_start(cb[:, :], I["blob"]).then_inc(blob_in, 16)
            for name, _ in LOADS:
                at_slot, _, reader = PLACE[name]
                if reader:
                    computed(sp, reader)
                slot, landed = ring[at_slot], ring_full[at_slot]
                if name[0] in ("branch", "wout"):
                    src = w_out if name[0] == "wout" else [I["w_br_a"], I["w_br_c"], I["w_br_b"], I["w_br_d"]][name[1]][0]
                    at = 2 * P * name[-1]
                    sp.dma_start(slot.rearrange("p (k n) -> p k n", k=2),
                                 src[at:at + 2 * P, :].rearrange("(k p) n -> p k n", p=P)
                                 ).then_inc(landed, 16)
                else:
                    if name[0] == "ada":
                        src, at = w_ada, 512 * name[1] + CW_ * name[2]
                    elif name[0] == "win":
                        src, at = w_in, CHUNKS[name[1]]
                    else:
                        src, at = w_gate, D * BRANCHES[name[1]][1] + CW_ * name[2]
                    sp.dma_start(slot.rearrange("p (k n) -> p k n", k=KD),
                                 src[:, at:at + CW_].rearrange("(k p) n -> p k n", p=P)
                                 ).then_inc(landed, 16)
                if name == ("ada", 1, 1):
                    sp.dma_start(xrow[:, 0, :], I["x_prompt"][0]).then_inc(x_in, 16)
                    sp.dma_start(xrow[:, 1:NT, :], I["x_sample"][0].rearrange("(t p) d -> p t d", p=P)
                                 ).then_inc(x_in, 16)
                if name == ("branch", 3, 1):
                    computed(sp, ("O", 4 * NT - 1))
                    sp.wait_ge(kv_out, 32)
                    sp.dma_start(x1[:, 0, :], I["x_prompt"][0]).then_inc(x_again, 16)
                    sp.dma_start(x1[:, 1:NT, :], I["x_sample"][0].rearrange("(t p) d -> p t d", p=P)
                                 ).then_inc(x_again, 16)
            wg = I["w_e_gate"].rearrange("l g e (p k) f -> (l g e) p k f", p=P)
            wu = I["w_e_up"].rearrange("l g e (p k) f -> (l g e) p k f", p=P)
            wd = I["w_e_down"].rearrange("l g e (k p) n -> (l g e) p k n", p=P)

            def load_one(dst, src, e, done):
                sp.dma_start(dst, src[e] if isinstance(e, int) else
                             src[bass.ds(e, 1)].rearrange("a p k n -> (a p) k n")).then_inc(done, 16)

            def load_up(e, s, done):
                load_one(wsets[s][0], wg, e, done)
                load_one(wsets[s][1], wu, e, done)

            def load_down(e, s, done):
                load_one(wsets[s][2], wd, e, done)

            def load_expert(e, s):
                load_up(e, s, w_full[s])
                load_down(e, s, wd_full[s])

            computed(sp, ("out", NT - 1))
            load_expert(0, 0)
            load_expert(1, 1)
            computed(sp, ("route", NT - 1))
            load_expert(2, 2)
            sp.wait_ge(h2_done, NT)
            load_expert(3, 3)
            for e in range(SETS, 2 * SETS):
                sp.wait_ge(gu_full, e + 1 - SETS)
                load_up(e, e - SETS, w_full[e - SETS])
                if e > SETS:
                    sp.wait_ge(dn_full, e - SETS)
                    load_down(e - 1, e - 1 - SETS, wd_full[e - 1 - SETS])
            with sp.Fori(2, EXPERTS // SETS) as i:
                for s in range(SETS):
                    sp.wait_ge(gu_full, i * SETS + (s + 1 - SETS))
                    load_up(i * SETS + s, s, w_full[s])
                    sp.wait_ge(dn_full, i * SETS + (s - SETS))
                    load_down(i * SETS + (s - 1), (s - 1) % SETS, wd_full[(s - 1) % SETS])
            sp.wait_ge(dn_full, EXPERTS - SETS)
            load_down(EXPERTS - 1, SETS - 1, wd_full[SETS - 1])
            n = n_further(sp)
            sp.wait_ge(dn_full, EXPERTS)
            with sp.If(n > 0):
                with sp.Fori(0, n) as i:
                    sp.wait_ge(dn_full, EXPERTS + i)
                    e = sp.value_load(ovi[0:1, bass.ds(i, 1)].bitcast(I32), min_val=0, max_val=EXPERTS - 1)
                    load_up(e, 0, ov_w)
                    load_down(e, 0, ov_w)
            sp.wait_ge(scatters_done, 1)
            for t in range(NT):
                for s in range(2):
                    sp.dma_start(fin_d[t][:, s, :], out_d[s * T + t * P:s * T + (t + 1) * P, :]
                                 ).then_inc(fin_in[t], 16)
            for t in range(NT):
                sp.wait_ge(fin_done, t + 1)
                dst = O[0][0] if t == 0 else O[1][0][(t - 1) * P:t * P, :]
                sp.dma_start(dst, x1[:, t, :]).then_inc(y_out, 16)
            sp.wait_ge(y_out, 16 * NT)
            sp.wait_ge(kv_out, 32)

        @block.gpsimd
        def _(pool):
            own = Own(pool, pool_own)
            own.put(pool.memset(vrows[1], 0.0))
            own.put(pool.memset(pwb[:], 0.0))
            pool.wait_ge(pool_own, 2)
            for name, src in (("b_ada", I["b_ada"][0].rearrange("(r c) -> r c", c=P)),
                              ("norm_mix", I["norm_mix"][0].rearrange("(r c) -> r c", c=P)),
                              ("b_gate", I["b_gate"][0].rearrange("(r c) -> r c", c=P)),
                              ("norm_ffn", I["norm_ffn"][0].rearrange("(r c) -> r c", c=P)),
                              ("pool_scale", I["pool_scale"][0].rearrange("(r c) -> r c", c=P)),
                              ("hyena_bias", I["hyena_bias"][0].rearrange("(r c) -> r c", c=P)),
                              ("hyena_conv", I["hyena_conv"][0].rearrange("k (r c) -> (k r) c", c=P)),
                              ("sconv_w", I["sconv_w"][0].rearrange("k (r c) -> (k r) c", c=P))):
                a, b = CV[name]
                pool.dma_start(vrows[0][a:b, :], src).then_inc(vecs_in, 16)
            pool.dma_start(zt, I["z"]).then_inc(filt_in, 16)
            pool.dma_start(f1s, I["hyena_f1"][0]).then_inc(filt_in, 16)
            pool.dma_start(f2s, I["hyena_f2"][0]).then_inc(filt_in, 16)
            pool.dma_start(f3s, I["hyena_f3"][0]).then_inc(filt_in, 16)
            pool.dma_start(decay, I["hyena_decay"][0].partition_broadcast(P)).then_inc(filt_in, 16)
            for g in range(4):
                a = 64 * (g % 2)
                pool.dma_start(pwb[a:a + 64, g // 2, a:a + 64], I["pool_w"][0, g]).then_inc(pw_in, 16)
            for c in range(4):
                computed(pool, ("adaT", c))
            pool.dma_start(RD[:, :], I["dft"]).then_inc(dft_in, 16)
            pool.dma_start(list_d.rearrange("(e t) a -> e (t a)", e=EXPERTS), I["lists"]).then_inc(list_init, 16)

            pool.dma_start(rpb_d, bass.AP(I["rpb"].tensor, RPB_PAD + 15,
                                          [[RPB_C, HEADS * RPB_R], [-1, GRID_W], [1, GRID_W]])).then_inc(rpb_out, 16)
            pool.wait_ge(rpb_out, 16)

            def load_bias(h, done):
                for half in range(2):
                    at = h * RPB_R + 1 - half
                    src = rpb_d[at:at + BROWS].rearrange("r q c -> q r c")
                    pool.dma_start(bias[h][64 * half:64 * half + 64, :].rearrange("p (s c) -> p s c", s=BROWS),
                                   src).then_inc(done, 16)

            def mask_bias(h):
                w = c_("window").unsqueeze(1).to_broadcast([P, BROWS, GRID_W])
                b = bias[h].rearrange("p (s c) -> p s c", s=BROWS)
                return pool.tensor_tensor(b, b, w, ALU.add)

            load_bias(0, bias01_in)
            load_bias(1, bias01_in)
            pool.wait_ge(blob_in, 16)
            pool.wait_ge(bias01_in, 64)
            mask_bias(0).then_inc(bias_ready01, 1)
            mask_bias(1).then_inc(bias_ready01, 1)
            pool.wait_ge(yb_done, 2)
            computed(pool, ("idft", 1))
            pool.dma_start(ckr, I["cache_k"][0, 0].rearrange("t h d -> t (h d)")).then_inc(cache_in, 16)
            pool.dma_start(cvr, I["cache_v"][0, 0].rearrange("t h d -> t (h d)")).then_inc(cache_in, 16)
            for h in range(2, HEADS):
                load_bias(h, bias_in)
            drained(pool, ("v", 0))
            pool.dma_start(O[3][0, 0].rearrange("t h d -> t (h d)"), vrow[:, 0, :]).then_inc(kv_out, 16)
            drained(pool, ("krow",))
            pool.dma_start(O[2][0, 0].rearrange("t h d -> t (h d)"), krow).then_inc(kv_out, 16)
            pool.wait_ge(bias_in, 32 * (HEADS - 2))
            for h in range(2, HEADS):
                mask_bias(h).then_inc(bias_ready, 1)
            def mod_rows():
                computed(pool, ("O", 4 * NT - 1))
                drained(pool, ("rows",))
                pool.dma_start(rows_d, junk[0:64, 0:P]).then_inc(rows_out, 16)
                pool.wait_ge(rows_out, 16)
                rv = rows_d.rearrange("(i k) c -> i (k c)", k=KD)
                for i in range(8):
                    pool.dma_start(rowb[:, i, :], rv[i].partition_broadcast(P)).then_inc(rows_in, 16)

            def router_weights():
                pool.dma_start(wroute[:, :, 0:NG], I["w_route_group"][0].rearrange("(k p) n -> p k n", p=P)
                               ).then_inc(route_in, 16)
                for g in range(NG):
                    pool.dma_start(wroute[:, :, NG + NE * g:NG + NE * (g + 1)],
                                   I["w_route_exp"][0, g].rearrange("(k p) n -> p k n", p=P)).then_inc(route_in, 16)
                pool.dma_start(rbias[:, 0:NG], I["b_route_group"][0].partition_broadcast(P)).then_inc(route_in, 16)
                pool.dma_start(rbias[:, NG:36], I["b_route_exp"][0].rearrange("g e -> (g e)").partition_broadcast(P)
                               ).then_inc(route_in, 16)

            for b in range(1, 4):
                if b == 3:
                    mod_rows()
                    router_weights()
                for dj in range(KD):
                    drained(pool, ("br", b, dj))
                    pool.tensor_tensor(merged[:, dj, :], merged[:, dj, :], gtmp, ALU.add).then_inc(merged_add, 1)
            for t in range(NT):
                k = 0 if t == 0 else 1
                pool.wait_ge(h2a_done, t + 1)
                if t == 0:
                    pool.wait_ge(rows_in, 128)
                pool.tensor_tensor(h2row[:, t % 2, :], h2row[:, t % 2, :], rowb[:, 6 + k, :], ALU.add
                                   ).then_inc(h2_done, 1)
                pool.wait_ge(h2_done, t + 1)
                for s in range(2):
                    pool.dma_start(hid_d[s * T + t * P:s * T + (t + 1) * P, :], h2row[:, t % 2, :]
                                   ).then_inc(h2_out[t % 2], 16)
            pool.dma_start(fin_n, I["norm_final"].partition_broadcast(P)).then_inc(nfin_in, 16)
            for t in range(NT):
                computed(pool, ("hT", t))
            for u in range(2, BUFS):
                own.put(pool.memset(xg[u], 0.0))
            def gather(e, b, idx_ap):
                pool.indirect_dma_start(xg[b], None, hid_d, bass.IndirectOffsetOnAxis(ap=idx_ap, axis=0),
                                        bounds_check=NPAIR - 1, oob_is_err=False).then_inc(xg_full[b], 16)

            def scatter(b, idx_ap):
                pool.indirect_dma_start(out_d, bass.IndirectOffsetOnAxis(ap=idx_ap, axis=0), yg[b], None,
                                        bounds_check=NPAIR - 1, oob_is_err=False).then_inc(y_sent[b], 16)

            idxu = idx.bitcast(U32)
            drained(pool, ("blocks",))
            pool.wait_ge(h2_out[0], 32 * 3)
            pool.wait_ge(h2_out[1], 32 * 2)
            pool.wait_ge(pool_own, own.n)
            for e in range(BUFS):
                gather(e, e, idxu[0:CAP, e:e + 1])

            pool.wait_ge(slots_done, 1)
            pool.wait_ge(list_init, 16)
            for n in range(2 * NT):
                pool.indirect_dma_start(list_d, bass.IndirectOffsetOnAxis(ap=slotu[:, n:n + 1].bitcast(U32), axis=0),
                                        c_("pair")[:, n:n + 1], None).then_inc(list_out, 16)

            def block_of(e, u):
                if e + BUFS <= EXPERTS:
                    pool.wait_ge(xT_full, e + 1)
                    gather(e + BUFS, u, idxu[0:CAP, e + BUFS:e + BUFS + 1])
                pool.wait_ge(dn_free, e + 1)
                scatter(u, idxu[0:CAP, e:e + 1])

            for e in range(EXPERTS):
                block_of(e, e % BUFS)
            def step_over():
                pool.sem_inc(pool_steps, 1)

            pool.wait_ge(list_out, 32 * NT)
            n = n_further(pool)
            for u in range(BUFS):
                pool.wait_ge(y_sent[u], 16 * EXPERTS // BUFS)
            pool.wait_ge(xg_full[0], 16 * (EXPERTS // BUFS + 1))
            with pool.If(n > 0):
                with pool.Fori(0, n) as i:
                    at = pool.value_load(ovi[0:1, bass.ds(i + NOV, 1)].bitcast(I32), min_val=0,
                                         max_val=EXPERTS * LIST - CAP)
                    pool.dma_start(idxo[0:CAP, 0:1], list_d[bass.ds(at, CAP), :]).then_inc(ov_idx_in, 16)
                    pool.wait_ge(ov_idx_ready, i + 1)
                    step_over()
                    gather(0, 0, idxo[0:CAP, 1:2].bitcast(U32))
                    pool.wait_ge(dn_free, i + (EXPERTS + 1))
                    step_over()
                    scatter(0, idxo[0:CAP, 1:2].bitcast(U32))
                    pool.wait_ge(y_sent[0], i * 16 + (16 * EXPERTS // BUFS + 16))
            pool.sem_inc(scatters_done, 1)
            for t in range(NT):
                a = fin_d[t][:, 0, :]
                pool.wait_ge(fin_sum, t + 1)
                pool.tensor_tensor(a, a, rowb[:, min(t, 1), :], ALU.mult).then_inc(fin_g2, 1)

        @block.scalar
        def _(act):
            own = Own(act, act_own)
            act.wait_ge(pool_own, 1)
            act.dma_start(vrows[1][0:8, :], I["c_ctx"].rearrange("(r c) -> r c", c=P)).then_inc(cond_in, 16)
            act.dma_start(vrows[1][8:16, :], I["c"][0].rearrange("(r c) -> r c", c=P)).then_inc(cond_in, 16)
            for n, name in enumerate(("hyena_fb1", "hyena_fb2", "hyena_freq")):
                act.dma_start(vrows[1][16 + n:17 + n, 0:64], I[name]).then_inc(cond_in, 16)


            def squares():
                act.wait_ge(x_in, 32)
                for t in range(NT):
                    own.put(act.activation(RA[:, D * t:D * (t + 1)], xrow[:, t, :], ACT.Square,
                                           accum_out=ssq[:, t:t + 1]))
                own.wait()
                act.activation(rms, ssq, ACT.Sqrt, bias=c_("eps"), scale=1.0 / D).then_inc(rms_done, 1)

            def vec(i):
                st = ("vec", i)
                computed(act, st)
                n = (CV if i == 0 else CW)["_"][1]
                frees(act.activation((colv if i == 0 else colw)[:, 0:n], ps(st)[:, 0:n], ACT.Copy), st)
                if i == 1:
                    drained(act, st)
                    act.activation(scT[:, :], colw[:, 0:16], ACT.Silu).then_inc(scT_done, 1)

            def p_tile(t):
                st = ("p", t)
                if t < 14:
                    s = SLOT[t]
                    if t == 10:
                        act.wait_ge(conv_done, 6)
                    computed(act, st)
                    own.put(act.activation(pt[:, s, CPAD:CPAD + TC], ps(st)[:, W0:W0 + TC], ACT.Copy))
                    frees(act.activation(pt[:, s, LPAD:LPAD + TL], ps(st)[:, W0 + TC:1024], ACT.Copy), st)
                else:
                    j = t - 14
                    dst = qT[:, j, :] if j < 4 else kT[:, j - 4, :]
                    computed(act, st)
                    frees(act.activation(dst, ps(st)[:, W0:1024], ACT.Copy), st)

            for st in STEPS:
                k = st[0]
                if k == "vec":
                    vec(st[1])
                elif k == "ada":
                    c = st[1]
                    computed(act, st)
                    frees(act.activation(ada_row(c), ps(st)[0:2, 0:512], ACT.Copy), st)
                    if c == 2:
                        squares()
                elif k in ("f1", "f2"):
                    n = 0 if k == "f1" else 1
                    act.wait_ge(sin_in, n + 1)
                    act.activation(sn[:, 2 + n, :], sn[:, 0, :], ACT.Sin).then_inc(sin_out, 1)
                elif k == "f3" and st[1] == 0:
                    act.wait_ge(filt_in, 80)
                    for t in range(NT):
                        act.activation(env[:, t, :], decay, ACT.Exp, scale=c_("negdist")[:, t:t + 1]
                                       ).then_inc(env_done, 1)
                elif k == "p":
                    p_tile(st[1])
                elif k == "uT":
                    computed(act, st)
                    c = st[1]
                    frees(act.activation(UF[:, :, P * c:P * (c + 1)],
                                         ps(st)[:, W0:1024].rearrange("p (t c) -> p t c", t=NT), ACT.Copy), st)
                elif k == "dft":
                    computed(act, st)
                    m = P if st[1] < 3 else NBC
                    if st[1] > 0:
                        act.wait_ge(ysp_done, st[1])
                    else:
                        act.wait_ge(ya_pooled, 4)
                    act.activation(hsp[0:m], ps(st)[0:m].rearrange("p (i c) -> p i c", i=2)[:, :, 256:512], ACT.Copy
                                   ).then_inc(hs_done, 1)
                elif k == "pw":
                    computed(act, st)
                    j = st[1]
                    frees(act.activation(yT[:, j, :], ps(st)[:, W0:1024], ACT.Copy,
                                         scale=v_("pool_scale")[:, j:j + 1]), st)
                elif k == "v":
                    computed(act, st)
                    frees(act.activation(vrow[:, st[1], :], ps(st)[:, 0:512], ACT.Copy), st)
                elif k == "krow":
                    computed(act, st)
                    act.wait_ge(padded_read, 1)
                    frees(act.activation(krow, ps(st)[:, 0:512], ACT.Copy), st)
                elif k == "ckT":
                    computed(act, st)
                    frees(act.activation(ckT.rearrange("p j t -> p (j t)"), ps(st)[:, 0:512], ACT.Copy), st)
                elif k == "S":
                    m = st[1]
                    act.wait_ge(exp_in, m + 1)
                    w = T if job(m)[1] else TC
                    act.activation(s_sb[:, m % 2, 0:w], s_sb[:, m % 2, 0:w], ACT.Exp,
                                   bias=negmax[:, m % 2:m % 2 + 1], accum_out=expsum[:, m % 2:m % 2 + 1]
                                   ).then_inc(exp_out, 1)
                elif k == "PT":
                    m = st[1]
                    computed(act, st)
                    if m >= 2:
                        computed(act, ("O", m // 2 - 1))
                    w = NT if job(m)[1] else 1
                    frees(act.activation(pT[:, m % 2, 0:w, :].rearrange("p k q -> p (k q)"), ps(st)[:, W0:W0 + w * P],
                                         ACT.Copy), st)
                elif k == "OT":
                    computed(act, st)
                    n = st[1]
                    frees(act.activation(qT[:, n // NT, P * (n % NT):P * (n % NT + 1)], ps(st)[:, 0:P], ACT.Copy), st)
                elif k == "gate":
                    b, dj = st[1:]
                    n = b * KD + dj
                    computed(act, st)
                    if n == 0:
                        act.wait_ge(padded_read, 1)
                    if n >= 2:
                        drained(act, ("br", (n - 2) // KD, (n - 2) % KD))
                    g = BRANCHES[b][1]
                    frees(act.activation(gate[:, n % 2, :], ps(st)[:, W0:1024], ACT.Sigmoid,
                                         bias=v_("b_gate")[:, KD * g + dj:KD * g + dj + 1]), st)
                elif k == "out":
                    t = st[1]
                    act.wait_ge(x1_done, t + 1)
                    own.link(act.activation(junk, x1[:, t, :], ACT.Square, accum_out=ssq[:, t:t + 1]))
                    act.activation(rms[:, t:t + 1], ssq[:, t:t + 1], ACT.Sqrt, bias=c_("eps"), scale=1.0 / D
                                   ).then_inc(ssq2_done, 1)
                elif k == "hT":
                    t = st[1]
                    computed(act, st)
                    frees(act.activation(hT[:, :, P * t:P * (t + 1)],
                                         ps(st)[:, :].rearrange("p (k t) -> p k t", k=KD), ACT.Copy), st)
                elif k == "pos":
                    act.wait_ge(gexp_in, 1)
                    act.activation(gx[1], gx[0], ACT.Exp)
                    act.activation(r5[4], r5[3], ACT.Exp).then_inc(gexp_out, 1)

            def turned(e, u, first=False):
                act.wait_ge(xT_full, e + 1)
                if not first:
                    act.wait_ge(gu_full, e - 1)
                act.activation(xgT[u % 2][:, :, 0:CAP], MX[:, :].rearrange("p (k b) -> p k b", k=KD)[:, :, 0:CAP],
                               ACT.Copy).then_inc(xT_free, 1)

            def silu(e, u, first=False):
                act.wait_ge(gu_full, e + 1)
                if not first:
                    act.wait_ge(gu_free, e - 1)
                act.activation(sil[u % 2][:, :, 0:CAP],
                               MG[:, 0:512].rearrange("p (f b) -> p f b", f=4)[:, 0:2, 0:CAP], ACT.Silu
                               ).then_inc(sil_done, 1)

            act.wait_ge(slots_done, 1)
            turned(0, 0, True)
            silu(0, 0, True)
            turned(1, 1, True)
            silu(1, 1, True)
            turned(2, 0)
            with act.Fori(1, EXPERTS // 2) as i:
                for u in range(2):
                    silu(i * 2 + u, u)
                    turned(i * 2 + (u + 1), u + 1)
            n = n_further(act)
            with act.If(n > 0):
                with act.Fori(0, n) as i:
                    turned(i + (EXPERTS + 1), 0)
                    silu(i + EXPERTS, 0)
            for n in range(NT + 2):
                if n < NT:
                    a = fin_d[n][:, 0, :]
                    act.wait_ge(fin_in[n], 32)
                    act.activation(a, a, ACT.Copy, scale=wA[:, n:n + 1]).then_inc(fin_first, 1)
                if n >= 2:
                    t = n - 2
                    act.wait_ge(fin_sq, t + 1)
                    own.link(act.activation(junk, x1[:, t, :], ACT.Square, accum_out=ssq[:, t:t + 1]))
                    act.activation(rms[:, t:t + 1], ssq[:, t:t + 1], ACT.Sqrt, bias=c_("eps"), scale=1.0 / D
                                   ).then_inc(fin_rms, 1)

        @block.vector
        def _(dve):
            own = Own(dve, dve_own)
            link, put = own.link, own.put
            ts, tt, stt = dve.tensor_scalar, dve.tensor_tensor, dve.scalar_tensor_tensor
            put(dve.memset(RP[:, :], 0.0))

            def normalise():
                dve.wait_ge(rms_done, 1)
                link(dve.reciprocal(rstd, rms))
                for t in range(NT):
                    ts(xrow[:, t, :], xrow[:, t, :], rstd[:, t:t + 1], None, ALU.mult).then_inc(xn_done, 1)

            def conv3(dst, src, w):
                n = WPAD - 2 * PAD
                link(ts(dst[:, PAD:PAD + n], src[:, PAD - 1:PAD - 1 + n], w[0], None, ALU.mult))
                link(stt(dst[:, PAD:PAD + n], src[:, PAD:PAD + n], w[1], dst[:, PAD:PAD + n], ALU.mult, ALU.add))
                return stt(dst[:, PAD:PAD + n], src[:, PAD + 1:PAD + 1 + n], w[2], dst[:, PAD:PAD + n], ALU.mult,
                           ALU.add)

            def both(ap):
                return (ap[:, CPAD:CPAD + TC], ap[:, LPAD:LPAD + TL])

            def sine_argument(n, st):
                fb, fr = colw[0:64, 16 + n:17 + n], colw[0:64, 18:19]
                x, q = sn[:, 0, :], sn[:, 1, :]
                computed(dve, st)
                if n == 0:
                    drained(dve, ("vec", 1))
                frees(ts(x, ps(st)[0:64, W0:1024], fb, fr, ALU.add, ALU.mult), st)
                drained(dve, st)
                magic = 1.5 * 2 ** 23
                link(ts(q, x, 1 / (2 * np.pi), magic, ALU.mult, ALU.add))
                link(ts(q, q, magic, None, ALU.subtract))
                c1 = 6.28125
                c2 = float(np.float32(np.round((2 * np.pi - c1) * 2 ** 21) / 2 ** 21))
                c3 = float(2 * np.pi - c1 - c2)
                for c in (c1, c2, c3):
                    link(stt(x, q, -c, x, ALU.mult, ALU.add))
                lim = float(np.nextafter(np.float32(np.pi), np.float32(0)))
                ts(x, x, lim, -lim, ALU.min, ALU.max).then_inc(sin_in, 1)

            def hyena_convs(c):
                w = v_("hyena_conv")

                def taps(r):
                    return [w[:, 6 * k + r:6 * k + r + 1] for k in range(3)]

                for t in (2 + c, 4 + c, 6 + c):
                    drained(dve, ("p", t))
                conv3(x0[:, c, :], pt[:, SLOT[2 + c], :], taps(c)).then_inc(conv_done, 1)
                conv3(cvt[:, 0, :], pt[:, SLOT[4 + c], :], taps(2 + c)).then_inc(conv_done, 1)
                conv3(cvt[:, 1, :], pt[:, SLOT[6 + c], :], taps(4 + c)).then_inc(conv_done, 1)
                dve.wait_ge(conv_done, 3 * c + 3)
                n = WPAD - 2 * PAD
                tt(uc[:, c, PAD:PAD + n], cvt[:, 0, PAD:PAD + n], cvt[:, 1, PAD:PAD + n], ALU.mult).then_inc(u_done, 1)
                dve.wait_ge(u_done, c + 1)

            def short_conv(c):
                for t in (8 + c, 10 + c, 12 + c):
                    drained(dve, ("p", t))
                xc, bg, cg = (pt[:, SLOT[t + c], :] for t in (8, 10, 12))
                w = v_("sconv_w")
                link(tt(xc, xc, cg, ALU.mult))
                link(conv3(cg, xc, [w[:, 2 * k + c:2 * k + c + 1] for k in range(3)]))
                for s, d in enumerate((yT[:, 4 + c, 0:TC], yT[:, 4 + c, TC:T])):
                    tt(d, both(bg)[s], both(cg)[s], ALU.mult).then_inc(yc_done, 1)

            def pool_mixer(j):
                drained(dve, ("p", j))
                u = pt[:, SLOT[j], :]
                A, B = cvt[:, 0, :], cvt[:, 1, :]
                if j:
                    dve.wait_ge(ya_pooled, 2)
                half = slice(64, P)
                link(tt(A[:, 1:WPAD], u[:, 0:WPAD - 1], u[:, 1:WPAD], ALU.add))
                if j == 0:
                    link(tt(B[half, 2:WPAD - 1], A[half, 1:WPAD - 2], A[half, 3:WPAD], ALU.add))
                    link(dve.tensor_copy(A[half, 8:WPAD - 8], B[half, 8:WPAD - 8]))
                else:
                    link(tt(B[:, 2:WPAD - 1], A[:, 1:WPAD - 2], A[:, 3:WPAD], ALU.add))
                    link(tt(A[:, 4:WPAD - 3], B[:, 2:WPAD - 5], B[:, 6:WPAD - 1], ALU.add))
                    link(tt(B[half, 8:WPAD - 7], A[half, 4:WPAD - 11], A[half, 12:WPAD - 3], ALU.add))
                    link(dve.tensor_copy(A[half, 8:WPAD - 8], B[half, 8:WPAD - 8]))
                e = c_("edge").rearrange("p (j s c) -> p j s c", j=2, s=4)
                for s, at in enumerate((CPAD, CPAD + TC - PAD, LPAD, LPAD + TL - PAD)):
                    put(tt(A[:, at:at + PAD], A[:, at:at + PAD], e[:, j, s, :], ALU.mult))
                own.wait()
                for s, d in enumerate((pooled[:, j, 0:TC], pooled[:, j, TC:T])):
                    stt(d, both(A)[s], c_("invwin")[:, j:j + 1], both(u)[s], ALU.mult, ALU.subtract
                        ).then_inc(ya_pooled, 1)

            def spectrum(kt):
                st = ("dft", kt)
                m = P if kt < 3 else NBC
                re, im = ps(st)[0:m, 0:256], ps(st)[0:m, 512:768]
                hr, hi = hsp[0:m, 0, :], hsp[0:m, 1, :]
                t4 = [tsp[0:m, i, :] for i in range(4)]
                yr, yi = (kt, 3 + kt) if kt < 3 else (6, 7)
                dve.wait_ge(hs_done, kt + 1)
                if kt > 0:
                    dve.wait_ge(ysp_done, kt)
                else:
                    dve.wait_ge(ya_pooled, 4)
                put(tt(t4[0], re, hr, ALU.mult))
                put(tt(t4[1], im, hi, ALU.mult))
                put(tt(t4[2], re, hi, ALU.mult))
                frees(tt(t4[3], im, hr, ALU.mult), st)
                drained(dve, st)
                put(tt(ysp[0:m, yr, :], t4[0], t4[1], ALU.subtract))
                tt(ysp[0:m, yi, :], t4[2], t4[3], ALU.add).then_inc(ysp_done, 1)

            def hyena_out(c):
                st = ("idft", c)
                computed(dve, st)
                outs = (yT[:, 2 + c, 0:TC], yT[:, 2 + c, TC:T])
                put(ts(outs[0], ps(st)[:, W0:W0 + TC], nrm[:, 2 * c:2 * c + 1], None, ALU.mult))
                frees(ts(outs[1], ps(st)[:, W0 + TC:1024], nrm[:, 2 * c + 1:2 * c + 2], None, ALU.mult), st)
                drained(dve, st)
                for s in range(2):
                    put(stt(outs[s], both(uc[:, c, :])[s], v_("hyena_bias")[:, c:c + 1], outs[s], ALU.mult, ALU.add))
                own.wait()
                put(tt(outs[0], outs[0], both(x0[:, c, :])[0], ALU.mult))
                tt(outs[1], outs[1], both(x0[:, c, :])[1], ALU.mult).then_inc(yb_done, 1)

            def softmax(m):
                h, t = job(m)
                st = ("S", m)
                s = s_sb[:, m % 2, :]
                computed(dve, st)
                if m == 2:
                    dve.wait_ge(bias_ready01, 2)
                if h == 2 and t == 1:
                    dve.wait_ge(bias_ready, HEADS - 2)
                if m >= 2:
                    computed(dve, ("PT", m - 2))
                if t == 0:
                    frees(ts(s[:, 0:TC], ps(st)[:, W0:W0 + TC], SCALE, None, ALU.mult), st)
                    w = TC
                else:
                    put(ts(s[:, 0:TC], ps(st)[:, W0:W0 + TC], SCALE, None, ALU.mult))
                    at = GRID_W * (6 - 2 * (t - 1))
                    frees(stt(s[:, TC:T], ps(st)[:, W0 + TC:1024], SCALE, bias[h][:, at:at + TL], ALU.mult, ALU.add),
                          st)
                    w = T
                drained(dve, st)
                link(dve.tensor_reduce(rowmax[:, m % 2:m % 2 + 1], s[:, 0:w], AX.X, ALU.max))
                ts(negmax[:, m % 2:m % 2 + 1], rowmax[:, m % 2:m % 2 + 1], -1.0, None, ALU.mult
                   ).then_inc(exp_in, 1)

            def attention_out(n):
                st = ("O", n)
                computed(dve, st)
                dve.wait_ge(exp_out, 2 * n + 2)
                if n:
                    drained(dve, ("O", n - 1))
                link(dve.reciprocal(rsum, expsum))
                if n >= 1:
                    computed(dve, ("OT", n - 1))
                put(ts(orow[:, 0:HD], ps(st)[:, 0:HD], rsum[:, 0:1], None, ALU.mult))
                frees(ts(orow[:, HD:P], ps(st)[:, HD:P], rsum[:, 1:2], None, ALU.mult), st)

            def merge(b, dj):
                st = ("br", b, dj)
                n = b * KD + dj
                computed(dve, st)
                drained(dve, ("gate", b, dj))
                if b == 0:
                    if n == 0:
                        computed(dve, ("idft", 1))
                    frees(tt(merged[:, dj, :], ps(st)[:, W0:1024], gate[:, n % 2, :], ALU.mult), st)
                    return
                if n > KD:
                    dve.wait_ge(merged_add, n - KD)
                frees(tt(gtmp, ps(st)[:, W0:1024], gate[:, n % 2, :], ALU.mult), st)

            def sum_half(c, h):
                sc = scT[:, :].rearrange("p (c k) -> p c k", c=2)
                w = loaded(dve, ("ada", c, h)).rearrange("p (k n) -> p k n", k=KD)
                computed(dve, PLACE["ada", c, h][2])
                if c > 4:
                    computed(dve, ("part", c - 1, h))
                sums = [apart[:, h, :], w[:, 0, :]]
                for kt in range(KD):
                    for kind in range(2):
                        if kt == 0:
                            own.wait()
                            put(ts(sums[kind], w[:, 0, :], sc[:, kind, 0:1], None, ALU.mult))
                        else:
                            dve.wait_ge(dve_own, own.n - 1)
                            put(stt(sums[kind], w[:, kt, :], sc[:, kind, kt:kt + 1], sums[kind], ALU.mult, ALU.add))
                own.wait()
                dve.sem_inc(ada_summed, 1)

            def ada_half(st):
                _, c, h = st
                computed(dve, st)
                at = 4 * c + 2 * h
                frees(tt(ada[:, 2 * at:2 * at + 4].rearrange("p (m k) -> p m k", k=2),
                         ps(st)[:, 0:4].rearrange("p (m k) -> p m k", k=2),
                         v_("b_ada")[:, at:at + 2].unsqueeze(2).to_broadcast([P, 2, 2]), ALU.add), st)

            def ada_columns(st):
                c = st[1]
                computed(dve, st)
                b = v_("b_ada")[:, 4 * c:4 * c + 4].unsqueeze(2).to_broadcast([P, 4, 2])
                if c == 0:
                    drained(dve, ("vec", 0))
                frees(tt(ada[:, 8 * c:8 * c + 8].rearrange("p (m k) -> p m k", k=2),
                         ps(st)[:, 0:8].rearrange("p (m k) -> p m k", k=2), b, ALU.add), st)

            def col(part, k):
                return ada[:, 16 * part:16 * part + 16].rearrange("p (m k) -> p k m", k=2)[:, k, :]

            for st in STEPS:
                k = st[0]
                if k in ("f1", "f2"):
                    sine_argument(0 if k == "f1" else 1, st)
                elif k == "f3":
                    computed(dve, st)
                    dve.wait_ge(env_done, NT)
                    ts_, n = ((0, 4) if st[1] == 0 else (4, 1))
                    frees(tt(UF[:, ts_:ts_ + n, 256:512],
                             ps(st)[:, 0:256 * n].rearrange("p (t c) -> p t c", t=n), env[:, ts_:ts_ + n, :],
                             ALU.mult), st)
                    drained(dve, st)
                    f = UF[:, ts_:ts_ + n, 256:512]
                    stt(env[:, ts_:ts_ + n, :], f, -1.0, f, ALU.mult, ALU.max).then_inc(abs_done, 1)
                elif k == "nrm":
                    computed(dve, st)
                    frees(dve.reciprocal(nrm, ps(st)[:, 0:4]), st)
                elif k == "adaT":
                    if st[1] == 2:
                        normalise()
                    ada_columns(st)
                    if st[1] == 3:
                        drained(dve, st)
                        for kind in range(2):
                            stt(a1[:, kind, :], col(1, kind), 1.0, v_("norm_mix"), ALU.add, ALU.mult
                                ).then_inc(mod1_done, 1)
                elif k == "part":
                    ada_half(st)
                elif k == "xT":
                    t = st[1]
                    kind = 0 if t == 0 else 1
                    dve.wait_ge(mod1_done, 2)
                    computed(dve, st)
                    for kt in range(KD):
                        ins = ts(hT[:, kt, P * t:P * (t + 1)], ps(st)[:, P * kt:P * (kt + 1)],
                                 a1[:, kind, kt:kt + 1], col(0, kind)[:, kt:kt + 1], ALU.mult, ALU.add)
                    frees(ins, st)
                elif k == "dft":
                    spectrum(st[1])
                elif k == "idft":
                    hyena_out(st[1])
                elif k == "p" and st[1] in (6, 7):
                    hyena_convs(st[1] - 6)
                elif k == "p" and st[1] in (12, 13):
                    short_conv(st[1] - 12)
                elif k == "p" and st[1] in (0, 1):
                    pool_mixer(st[1])
                    if st[1] == 1:
                        dve.wait_ge(ya_pooled, 4)
                        dve.wait_ge(yc_done, 4)
                        dve.memset(small[:, 54:55], 0.0).then_inc(padded_read, 1)
                elif k == "S":
                    softmax(st[1])
                elif k == "O":
                    attention_out(st[1])
                elif k == "br":
                    n = st[1] * KD + st[2]
                    if n in HALVES:
                        sum_half(*HALVES[n])
                    merge(st[1], st[2])
                elif k == "rows":
                    mv = mod[:, :].rearrange("p (i m) -> p i m", m=KD)
                    drained(dve, ("part", 11, 0))
                    drained(dve, ("part", 11, 1))
                    for kind in range(2):
                        put(dve.tensor_copy(mv[:, kind, :], col(5, kind)))
                        put(dve.tensor_copy(mv[:, 2 + kind, :], col(2, kind)))
                        put(stt(mv[:, 4 + kind, :], col(4, kind), 1.0, v_("norm_ffn"), ALU.add, ALU.mult))
                        put(dve.tensor_copy(mv[:, 6 + kind, :], col(3, kind)))
                    own.wait()
                    dve.sem_inc(mod_done, 1)
                    computed(dve, st)
                    frees(dve.tensor_copy(junk[0:64, 0:P], ps(st)[0:64, 0:P]), st)
                elif k == "out":
                    t = st[1]
                    kind = 0 if t == 0 else 1
                    computed(dve, st)
                    if t == 0:
                        dve.wait_ge(rows_in, 128)
                        dve.wait_ge(x_again, 32)
                        dve.wait_ge(rows_out, 16)
                    tmp = h2row[:, t % 2, :]
                    if t >= 2:
                        dve.wait_ge(h2_out[t % 2], 32 * (t // 2))
                        computed(dve, ("hT", t - 2))
                    frees(tt(tmp, ps(st)[:, :], rowb[:, 2 + kind, :], ALU.mult), st)
                    drained(dve, st)
                    tt(x1[:, t, :], x1[:, t, :], tmp, ALU.add).then_inc(x1_done, 1)
                    dve.wait_ge(x1_done, t + 1)
                    dve.wait_ge(ssq2_done, t + 1)
                    link(dve.reciprocal(rstd[:, t:t + 1], rms[:, t:t + 1]))
                    stt(tmp, x1[:, t, :], rstd[:, t:t + 1], rowb[:, 4 + kind, :], ALU.mult, ALU.mult
                        ).then_inc(h2a_done, 1)
                elif k == "route":
                    t = st[1]
                    computed(dve, st)
                    dve.wait_ge(route_in, 16 * 7)
                    frees(tt(lg[:, t, :], ps(st)[:, 0:36], rbias, ALU.add), st)
                elif k == "pos":
                    gl = lg[:, :, 0:NG]
                    el = lg[:, :, NG:36].rearrange("p t (g e) -> p t g e", g=NG)
                    drained(dve, ("route", NT - 1))

                    def first_max(vals, top, n, ids, scratch, out):
                        link(dve.tensor_reduce(top, vals, AX.X, ALU.max))
                        link(tt(out, vals, top.unsqueeze(2).to_broadcast([P, NT, n]), ALU.is_equal))
                        idb = ids.unsqueeze(1).to_broadcast([P, NT, n])
                        link(tt(scratch, out, idb, ALU.mult))
                        link(dve.tensor_reduce(r5[11], scratch, AX.X, ALU.min))
                        link(tt(out, r5[11].unsqueeze(2).to_broadcast([P, NT, n]), idb, ALU.is_equal))

                    first_max(gl, r5[0], NG, c_("gid"), gx[0], gx[2])
                    link(tt(gx[0], gl, r5[0].unsqueeze(2).to_broadcast([P, NT, NG]), ALU.subtract))
                    for t in range(NT):
                        put(tt(m32[:, t], el[:, t], gx[2][:, t, :].unsqueeze(2).to_broadcast([P, NG, NE]), ALU.mult))
                    own.wait()
                    link(tt(ex[0], m32[:, :, 0, :], m32[:, :, 1, :], ALU.add))
                    link(tt(ex[0], ex[0], m32[:, :, 2, :], ALU.add))
                    link(tt(ex[0], ex[0], m32[:, :, 3, :], ALU.add))
                    first_max(ex[0], r5[1], NE, c_("eid"), ex[4], ex[1])
                    link(stt(ex[3], ex[1], -3e38, ex[0], ALU.mult, ALU.add))
                    first_max(ex[3], r5[2], NE, c_("eid"), ex[4], ex[2])
                    tt(r5[3], r5[2], r5[1], ALU.subtract).then_inc(gexp_in, 1)
                    for t in range(NT):
                        g = gx[2][:, t, :].unsqueeze(2).to_broadcast([P, NG, NE])
                        put(tt(selA[:, t], ex[1][:, t, :].unsqueeze(1).to_broadcast([P, NG, NE]), g, ALU.mult))
                        put(tt(selB[:, t], ex[2][:, t, :].unsqueeze(1).to_broadcast([P, NG, NE]), g, ALU.mult))
                    own.wait()
                    flat = "p t g e -> p (t g e)"
                    tt(m32.rearrange(flat), selA.rearrange(flat), selB.rearrange(flat), ALU.add
                       ).then_inc(mask_done, 1)
                    dve.wait_ge(gexp_out, 1)
                    link(dve.tensor_reduce(r5[5], gx[1], AX.X, ALU.add))
                    link(ts(r5[6], r5[4], 1.0, None, ALU.add))
                    link(tt(r5[7], r5[5], r5[6], ALU.mult))
                    link(dve.reciprocal(wA, r5[7]))
                    put(tt(wB, wA, r5[4], ALU.mult))
                    for s, sel in enumerate((selA, selB)):
                        ids = c_("pair")[:, NT * s:NT * (s + 1)].unsqueeze(2).to_broadcast([P, NT, EXPERTS])
                        to = idsel[:, NT * s:NT * (s + 1), :]
                        sel3 = sel.rearrange("p t g e -> p t (g e)")
                        link(ts(to, ids, -2.0 * NPAIR, None, ALU.add))
                        put(tt(to, to, sel3, ALU.mult))
                    computed(dve, st)
                    frees(dve.tensor_copy(posb, ps(st)[:, 0:160].rearrange("p (t n) -> p t n", t=NT)), st)
                    drained(dve, st)
                    for s, sel in enumerate((selA, selB)):
                        sel3 = sel.rearrange("p t g e -> p t (g e)")
                        link(tt(ranked, sel3, posb, ALU.mult))
                        link(dve.tensor_reduce(rankf[:, NT * s:NT * (s + 1)], ranked, AX.X, ALU.add))
                    for n in range(2 * NT):
                        put(ts(atplace[:, n, :], c_("place"), rankf[:, n:n + 1], None, ALU.is_equal))
                    own.wait()
                    dve.sem_inc(places_done, 1)
                elif k == "count":
                    computed(dve, st)
                    nb = BLOCKS - 1
                    frees(tt(fl5[0:32, 0:nb], ps(st)[0:32, 0:1].to_broadcast([32, nb]), c_("thr", 32), ALU.is_gt), st)
                    drained(dve, st)
                    dve.tensor_reduce(cnt[0:32, 0:1], fl5[0:32, 0:nb], AX.X, ALU.add).then_inc(flags_done, 1)
                elif k == "further":
                    computed(dve, st)
                    nb = BLOCKS - 1
                    link(dve.tensor_copy(cnt[0:32, 1:2], ps(st)[0:32, 0:1]))
                    frees(dve.tensor_copy(ovr[0:1, 2 * NOV:2 * NOV + 1], ps(st)[0:1, 8:9]), st)
                    for b in range(nb):
                        link(ts(ovs[0:32, NOV * b:NOV * (b + 1)], c_("iota", 32), float(b), cnt[0:32, 1:2],
                                ALU.subtract, ALU.is_equal))
                        ts(ovs[0:32, NOV * b:NOV * (b + 1)], ovs[0:32, NOV * b:NOV * (b + 1)], fl5[0:32, b:b + 1],
                           None, ALU.mult).then_inc(sel_done, 1)
                elif k == "lists":
                    computed(dve, st)
                    frees(dve.tensor_copy(ovr[0:1, 0:2 * NOV], ps(st)[0:1, 0:2 * NOV]), st)
                    drained(dve, st)
                    drained(dve, ("further",))
                    dve.tensor_copy(ovi[0:1, :].bitcast(I32), ovr[0:1, :]).then_inc(list_ready, 1)
                    for s, sel in enumerate((selA, selB)):
                        sel3 = sel.rearrange("p t g e -> p t (g e)")
                        link(tt(ranked, sel3, c_("slot0").unsqueeze(1).to_broadcast([P, NT, EXPERTS]), ALU.mult))
                        link(dve.tensor_reduce(slotf[:, NT * s:NT * (s + 1)], ranked, AX.X, ALU.add))
                    link(tt(slotf, slotf, rankf, ALU.add))
                    dve.tensor_copy(slotu.bitcast(U32), slotf).then_inc(slots_done, 1)
                elif k == "blocks":
                    put(dve.tensor_copy(idx.bitcast(U32)[:, EXPERTS:EXPERTS + 1], c_("nopair")))
                    computed(dve, st)
                    link(ts(idxf[0:CAP, :], ps(st)[0:CAP, 0:EXPERTS], 2.0 * NPAIR, None, ALU.add))
                    frees(dve.tensor_copy(idx.bitcast(U32)[0:CAP, 0:EXPERTS], idxf[0:CAP, :]), st)

            def hidden(e, u, first=False):
                dve.wait_ge(sil_done, e + 1)
                if not first:
                    dve.wait_ge(dn_full, e - 1)
                tt(hid[u % 2][:, :, 0:CAP], MG[:, 512:1024].rearrange("p (f b) -> p f b", f=4)[:, 0:2, 0:CAP],
                   sil[u % 2][:, :, 0:CAP], ALU.mult).then_inc(gu_free, 1)

            def result(e, u, i, first=False):
                dve.wait_ge(dn_full, e + 1)
                if not first:
                    dve.wait_ge(y_sent[u], i * 16)
                dve.tensor_copy(yg[u], MD[0:CAP, :]).then_inc(dn_free, 1)

            hidden(0, 0, True)
            for e in range(1, BUFS):
                hidden(e, e % 2, e < 2)
                result(e - 1, e - 1, 0, True)
            hidden(BUFS, 0)
            result(BUFS - 1, BUFS - 1, 0, True)
            with dve.Fori(1, EXPERTS // BUFS - 1) as i:
                for u in range(BUFS):
                    hidden(i * BUFS + (u + 1), (u + 1) % 2)
                    result(i * BUFS + u, u, i)
            last = EXPERTS // BUFS - 1
            for u in range(BUFS):
                if u < BUFS - 1:
                    hidden(last * BUFS + u + 1, (u + 1) % 2)
                result(last * BUFS + u, u, last)
            n = n_further(dve)
            with dve.If(n > 0):
                with dve.Fori(0, n) as i:
                    dve.wait_ge(ov_idx_in, i * 16 + 16)
                    dve.tensor_copy(idxo[0:CAP, 1:2].bitcast(U32), idxo[0:CAP, 0:1]).then_inc(ov_idx_ready, 1)
                    hidden(i + EXPERTS, 0)
                    dve.wait_ge(dn_full, i + (EXPERTS + 1))
                    dve.wait_ge(y_sent[0], i * 16 + 16 * EXPERTS // BUFS)
                    dve.tensor_copy(yg[0], MD[0:CAP, :]).then_inc(dn_free, 1)
            dve.wait_ge(nfin_in, 16)
            for n in range(NT + 2):
                if n < NT:
                    a, b = fin_d[n][:, 0, :], fin_d[n][:, 1, :]
                    dve.wait_ge(fin_first, n + 1)
                    stt(a, b, wB[:, n:n + 1], a, ALU.mult, ALU.add).then_inc(fin_sum, 1)
                if 0 <= n - 1 < NT:
                    t = n - 1
                    dve.wait_ge(fin_g2, t + 1)
                    tt(x1[:, t, :], x1[:, t, :], fin_d[t][:, 0, :], ALU.add).then_inc(fin_sq, 1)
                if n >= 2:
                    t = n - 2
                    dve.wait_ge(fin_rms, t + 1)
                    link(dve.reciprocal(rstd[:, t:t + 1], rms[:, t:t + 1]))
                    stt(x1[:, t, :], x1[:, t, :], rstd[:, t:t + 1], fin_n, ALU.mult, ALU.mult).then_inc(fin_done, 1)

        @block.tensor
        def _(pe):
            mm = pe.matmul

            def wide(ps_, lhsT, rhs, start, stop, m=P):
                mm(ps_[0:m, W0:W0 + TC], lhsT, rhs[:, 0:TC], start=start, stop=stop)
                return mm(ps_[0:m, W0 + TC:1024], lhsT, rhs[:, TC:T], start=start, stop=stop)

            def turn(out, in_, n=P):
                return pe.transpose(out, in_, ident[0:n, 0:n])

            def attention_s(m):
                h, t = job(m)
                a, j = HD * (h % 2), h // 2
                q = qT[a:a + HD, j, P * t:P * (t + 1)]
                keys = kT[a:a + HD, j, 0:TC] if t == 0 else ckT[a:a + HD, j, :]
                ins = mm(p_[:, W0:W0 + TC], q, keys, start=True, stop=True)
                if t:
                    ins = mm(p_[:, W0 + TC:1024], q, kT[a:a + HD, j, TC:T], start=True, stop=True)
                return ins

            for n, st in enumerate(STEPS):
                k, p_ = st[0], ps(st)
                if n >= 4:
                    drained(pe, STEPS[n - 4])
                if k == "vec":
                    if st[1] == 0:
                        pe.wait_ge(vecs_in, 16 * 8)
                    else:
                        pe.wait_ge(blob_in, 16)
                        pe.wait_ge(cond_in, 16 * 5)
                    nr = (CV if st[1] == 0 else CW)["_"][1]
                    ins = turn(p_[:, 0:nr], vrows[st[1]][0:nr, :], nr)
                elif k == "f1":
                    pe.wait_ge(filt_in, 80)
                    ins = wide(p_, f1s, zt, True, True, 64)
                elif k == "f2":
                    pe.wait_ge(sin_out, 1)
                    ins = wide(p_, f2s, sn[:, 2, :], True, True, 64)
                elif k == "f3":
                    pe.wait_ge(sin_out, 2)
                    for i, t in enumerate(range(4) if st[1] == 0 else (4,)):
                        ins = mm(p_[:, 256 * i:256 * (i + 1)], sn[:, 3, P * t:P * (t + 1)], f3s, start=True, stop=True)
                elif k == "nrm":
                    pe.wait_ge(abs_done, 2)
                    for c in range(2):
                        for kind, tl in enumerate(((0,), (1, 2, 3, 4))):
                            for t in tl:
                                ins = mm(p_[:, 2 * c + kind:2 * c + kind + 1], env[:, t, P * c:P * (c + 1)],
                                         c_("ones")[:, 0:1], start=(t == tl[0]), stop=(t == tl[-1]))
                elif k == "part":
                    pe.wait_ge(ada_summed, 2 * (st[1] - 4) + st[2] + 1)
                    sums = [apart[:, st[2], :], loaded(pe, loads_of(st)[0])[:, 0:CW_]]
                    for m in range(CW_ // P):
                        for kind in range(2):
                            ins = mm(p_[:, 2 * m + kind:2 * m + kind + 1], sums[kind][:, P * m:P * (m + 1)],
                                     c_("ones")[:, 0:1], start=True, stop=True)
                elif k == "ada":
                    if st[1] == 0:
                        pe.wait_ge(scT_done, 1)
                    sc = scT[:, :].rearrange("p (c k) -> p k c", c=2)
                    for name in loads_of(st):
                        w = loaded(pe, name).rearrange("p (k n) -> p k n", k=KD)
                        for kt in range(KD):
                            ins = mm(p_[0:2, CW_ * name[2]:CW_ * (name[2] + 1)], sc[:, kt, :], w[:, kt, :],
                                     start=(kt == 0), stop=(kt == KD - 1))
                elif k == "adaT":
                    drained(pe, ("ada", st[1]))
                    for m in range(4):
                        ins = turn(p_[:, 2 * m:2 * m + 2], ada_row(st[1])[:, P * m:P * (m + 1)], 2)
                elif k == "xT":
                    t = st[1]
                    pe.wait_ge(xn_done, t + 1)
                    for kt in range(KD):
                        ins = turn(p_[:, P * kt:P * (kt + 1)], xrow[:, t, P * kt:P * (kt + 1)])
                elif k == "p":
                    t = st[1]
                    w = loaded(pe, loads_of(st)[-1]).rearrange("p (k n) -> p k n", k=KD)
                    at = P * t - CHUNKS[CHUNK_OF[t]]
                    if t == 2:
                        for t_ in range(NT):
                            drained(pe, ("xT", t_))
                    for kt in range(KD):
                        ins = wide(p_, w[:, kt, at:at + P], hT[:, kt, :], kt == 0, kt == KD - 1)
                elif k == "uT":
                    c = st[1]
                    pe.wait_ge(u_done, c + 1)
                    for t in range(NT):
                        at = CPAD if t == 0 else LPAD + P * (t - 1)
                        ins = turn(p_[:, W0 + P * t:W0 + P * (t + 1)], uc[:, c, at:at + P])
                elif k == "dft":
                    kt = st[1]
                    if kt == 0:
                        pe.wait_ge(dft_in, 16)
                        drained(pe, ("uT", 1))
                    for im in range(2):
                        if kt < 3:
                            for t in range(4):
                                a = NBL * im + P * kt
                                ins = mm(p_[:, 512 * im:512 * (im + 1)], FLt[:, t, a:a + P], UF[:, 1 + t, :],
                                         start=(t == 0), stop=(t == 3))
                        else:
                            ins = mm(p_[0:NBC, 512 * im:512 * (im + 1)], FC[:, NBC * im:NBC * (im + 1)], UF[:, 0, :],
                                     start=True, stop=True)
                elif k == "idft":
                    c = st[1]
                    pe.wait_ge(ysp_done, 4)
                    for i in range(2):
                        mm(p_[:, W0:W0 + TC], ysp[0:NBC, 6 + i, P * c:P * (c + 1)], IC[0:NBC, i, :],
                           start=(i == 0), stop=(i == 1))
                    for i in range(6):
                        ins = mm(p_[:, W0 + TC:1024], ysp[:, i, P * c:P * (c + 1)], IL[:, i, :],
                                 start=(i == 0), stop=(i == 5))
                elif k == "pw":
                    pe.wait_ge(ya_pooled, 4)
                    pe.wait_ge(pw_in, 64)
                    ins = wide(p_, pwb[:, st[1], :], pooled[:, st[1], :], True, True)
                elif k == "v":
                    t = st[1]
                    for h, name in enumerate(loads_of(st)):
                        w = loaded(pe, name).rearrange("p (k n) -> p k n", k=KD)
                        for kt in range(KD):
                            ins = mm(p_[:, CW_ * h:CW_ * (h + 1)], hT[:, kt, P * t:P * (t + 1)], w[:, kt, :],
                                     start=(kt == 0), stop=(kt == KD - 1))
                elif k == "krow":
                    for j in range(4):
                        drained(pe, ("p", 18 + j))
                        ins = turn(p_[:, P * j:P * (j + 1)], kT[:, j, 0:P])
                elif k == "ckT":
                    pe.wait_ge(cache_in, 32)
                    for j in range(4):
                        ins = turn(p_[:, P * j:P * (j + 1)], ckr[:, P * j:P * (j + 1)])
                elif k == "S":
                    if st[1] == 0:
                        drained(pe, ("ckT",))
                    ins = attention_s(st[1])
                elif k == "PT":
                    m = st[1]
                    pe.wait_ge(exp_out, m + 1)
                    for i in range(NT if job(m)[1] else 1):
                        ins = turn(p_[:, W0 + P * i:W0 + P * (i + 1)], s_sb[:, m % 2, P * i:P * (i + 1)])
                elif k == "O":
                    m0 = 2 * st[1]
                    t = job(m0)[1]
                    for m in (m0, m0 + 1):
                        drained(pe, ("PT", m))
                        h = job(m)[0]
                        nk = NT if t else 1
                        for i in range(nk):
                            if t == 0:
                                v = vrow[:, 0, HD * h:HD * (h + 1)]
                            elif i == 0:
                                v = cvr[:, HD * h:HD * (h + 1)]
                            else:
                                v = vrow[:, i, HD * h:HD * (h + 1)]
                            ins = mm(p_[:, HD * (m % 2):HD * (m % 2 + 1)], pT[:, m % 2, i, :], v, start=(i == 0),
                                     stop=(i == nk - 1))
                elif k == "OT":
                    drained(pe, ("O", st[1]))
                    ins = turn(p_[:, 0:P], orow)
                elif k == "gate":
                    b, dj = st[1:]
                    w = loaded(pe, loads_of(st)[-1]).rearrange("p (k n) -> p k n", k=KD)
                    at = P * (dj % 2)
                    for kt in range(KD):
                        ins = wide(p_, w[:, kt, at:at + P], hT[:, kt, :], kt == 0, kt == KD - 1)
                elif k == "br":
                    b, dj = st[1:]
                    kb = BRANCHES[b][2]
                    if dj == 0:
                        if b == 0:
                            drained(pe, ("pw", 1))
                        elif b == 1:
                            pe.wait_ge(yc_done, 4)
                        elif b == 2:
                            pe.wait_ge(yb_done, 2)
                        else:
                            drained(pe, ("OT", 4 * NT - 1))
                    for i in range(kb):
                        if i % 2 == 0:
                            w = loaded(pe, ("branch", b, i // 2)).rearrange("p (k n) -> p k n", k=2)
                        src = (yaT, ycT, ybT, qT)[b][:, min(i, 1) if b < 3 else i, :]
                        ins = wide(p_, w[:, i % 2, P * dj:P * (dj + 1)], src, i == 0, i == kb - 1)
                elif k == "rows":
                    pe.wait_ge(mod_done, 1)
                    ins = turn(p_[0:64, 0:P], mod[:, 0:64])
                elif k == "out":
                    t = st[1]
                    if t == 0:
                        pe.wait_ge(merged_add, 3 * KD)
                    for kt in range(KD):
                        if kt % 2 == 0:
                            w = loaded(pe, ("wout", kt // 2)).rearrange("p (k n) -> p k n", k=2)
                        for half in range(2):
                            ins = mm(p_[:, 512 * half:512 * (half + 1)], merged[:, kt, P * t:P * (t + 1)],
                                     w[:, kt % 2, 512 * half:512 * (half + 1)], start=(kt == 0), stop=(kt == KD - 1))
                elif k == "hT":
                    t = st[1]
                    pe.wait_ge(h2_done, t + 1)
                    for kt in range(KD):
                        ins = turn(p_[:, P * kt:P * (kt + 1)], h2row[:, t % 2, P * kt:P * (kt + 1)])
                elif k == "route":
                    t = st[1]
                    drained(pe, ("hT", t))
                    pe.wait_ge(route_in, 16 * 7)
                    for kt in range(KD):
                        ins = mm(p_[:, 0:36], hT[:, kt, P * t:P * (t + 1)], wroute[:, kt, :], start=(kt == 0),
                                 stop=(kt == KD - 1))
                elif k == "pos":
                    pe.wait_ge(mask_done, 1)
                    for t in range(NT):
                        for t2 in range(t + 1):
                            ins = mm(p_[:, EXPERTS * t:EXPERTS * (t + 1)], c_("before") if t2 == t else c_("ones"),
                                     m32[:, t2].rearrange("p g e -> p (g e)"), start=(t2 == 0), stop=(t2 == t))
                elif k == "count":
                    for t in range(NT):
                        ins = mm(p_[0:EXPERTS, 0:1], m32[:, t].rearrange("p g e -> p (g e)"), c_("ones")[:, 0:1],
                                 start=(t == 0), stop=(t == NT - 1))
                elif k == "further":
                    pe.wait_ge(flags_done, 1)
                    mm(p_[0:32, 0:1], c_("before")[0:32, 0:32], cnt[0:32, 0:1], start=True, stop=True)
                    ins = mm(p_[0:1, 8:9], cnt[0:32, 0:1], c_("ones")[0:32, 0:1], start=True, stop=True)
                elif k == "lists":
                    nb = BLOCKS - 1
                    pe.wait_ge(sel_done, nb)
                    ids = c_("blk", 32).rearrange("p (b i) -> p b i", i=2)
                    for i in range(2):
                        for b in range(nb):
                            ins = mm(p_[0:1, NOV * i:NOV * (i + 1)], ids[:, b, i:i + 1],
                                     ovs[0:32, NOV * b:NOV * (b + 1)], start=(b == 0), stop=(b == nb - 1))
                elif k == "blocks":
                    pe.wait_ge(places_done, 1)
                    for i in range(2 * NT):
                        ins = mm(p_[0:CAP, 0:EXPERTS], atplace[:, i, :], idsel[:, i, :], start=(i == 0),
                                 stop=(i == 2 * NT - 1))
                ins.then_inc(psum_full[n % 4], 1)

            for st in STEPS[-4:]:
                drained(pe, st)

            def turn_x(e, u, arrivals):
                pe.wait_ge(xg_full[u], arrivals)
                if not isinstance(e, int) or e:
                    pe.wait_ge(xT_free, e)
                for kt in range(KD):
                    ins = turn(MX[:, P * kt:P * kt + CAP], xg[u].rearrange("r (p k) -> r k p", k=KD)[:, kt, :], CAP)
                ins.then_inc(xT_full, 1)

            def up(e, u, s, arrived, weights, turned):
                pe.wait_ge(arrived, weights)
                pe.wait_ge(xT_free, turned)
                if not isinstance(e, int) or e:
                    pe.wait_ge(gu_free, e)
                for g, w in enumerate(wsets[s][0:2]):
                    for f in range(2):
                        for kt in range(KD):
                            ins = mm(MG[:, 512 * g + P * f:512 * g + P * f + CAP], w[:, kt, P * f:P * (f + 1)],
                                     xgT[u][:, kt, 0:CAP], start=(kt == 0), stop=(kt == KD - 1))
                ins.then_inc(gu_full, 1)

            def down(e, u, s, arrived, weights):
                pe.wait_ge(arrived, weights)
                pe.wait_ge(gu_free, e + 1)
                if not isinstance(e, int) or e:
                    pe.wait_ge(dn_free, e)
                for half in range(2):
                    for f in range(2):
                        ins = mm(MD[0:CAP, 512 * half:512 * (half + 1)], hid[u][:, f, 0:CAP],
                                 wsets[s][2][:, f, 512 * half:512 * (half + 1)], start=(f == 0), stop=(f == 1))
                ins.then_inc(dn_full, 1)

            turn_x(0, 0, 16)
            for e in range(SETS):
                up(e, e % 2, e, w_full[e], 32, e + 1)
                turn_x(e + 1, (e + 1) % BUFS, 16 * ((e + 1) // BUFS + 1))
                if e:
                    down(e - 1, (e - 1) % 2, e - 1, wd_full[e - 1], 16)
            with pe.Fori(1, EXPERTS // SETS) as i:
                for s in range(SETS):
                    e = i * SETS + s
                    up(e, s % 2, s, w_full[s], i * 32 + 32, e + 1)
                    turn_x(e + 1, (s + 1) % BUFS, i * 16 + 16 * ((s + 1) // BUFS + 1))
                    down(i * SETS + (s - 1), (s - 1) % 2, (s - 1) % SETS, wd_full[(s - 1) % SETS],
                         i * 16 + (16 if s else 0))
            down(EXPERTS - 1, (EXPERTS - 1) % 2, SETS - 1, wd_full[SETS - 1], 16 * EXPERTS // SETS)
            n = n_further(pe)
            with pe.If(n > 0):
                with pe.Fori(0, n) as i:
                    turn_x(i + (EXPERTS + 1), 0, i * 16 + 16 * (EXPERTS // BUFS + 2))
                    up(i + EXPERTS, 0, 0, ov_w, i * 48 + 48, i + (EXPERTS + 2))
                    down(i + EXPERTS, 0, 0, ov_w, i * 48 + 48)

    return nc


_INS = ["x_prompt", "x_sample", "cache_k", "cache_v", "c", "c_ctx", "w_ada", "b_ada", "norm_mix", "w_in", "w_gate",
        "b_gate", "pool_w", "pool_scale", "hyena_conv", "hyena_f1", "hyena_fb1", "hyena_f2", "hyena_fb2", "hyena_f3",
        "hyena_freq", "hyena_decay", "hyena_bias", "sconv_w", "w_br_a", "w_br_b", "w_br_c", "w_br_d", "w_out",
        "norm_ffn", "w_route_group", "b_route_group", "w_route_exp", "b_route_exp", "w_e_gate", "w_e_up", "w_e_down",
        "norm_final"]
_OUTS = [(1, TC, D), (1, TL, D), (1, 1, TC, HEADS, HD), (1, 1, TC, HEADS, HD)]


def kernel(**inputs):
    import numpy as _np
    import concourse.bacc as _bacc
    from concourse import mybir as _mybir
    from concourse.bass_utils import run_bass_kernel_spmd as _run

    nc = _bacc.Bacc("TRN2", target_bir_lowering=False, num_devices=1)
    arrays, aps = {}, {}
    given = {name: _np.ascontiguousarray(inputs[name]) for name in _INS}
    edge = _np.zeros(RPB_PAD, _np.float32)
    given["rpb"] = _np.concatenate([edge, _np.ascontiguousarray(inputs["na_rpb"]).reshape(-1), edge])
    given.update(constants())
    for name, a in given.items():
        arrays[f"in_{name}"] = a
        aps[name] = nc.dram_tensor(f"in_{name}", a.shape, _mybir.dt.from_np(a.dtype), kind="ExternalInput").ap()
    outs = [nc.dram_tensor(f"out_{i}", shape, F32, kind="ExternalOutput").ap() for i, shape in enumerate(_OUTS)]
    build(nc, aps, outs)
    r = _run(nc, [arrays], core_ids=[0])
    return tuple(r.results[0][f"out_{i}"] for i in range(len(_OUTS)))
```
